# Optimizing a Trainium2 kernel written in Bass

```python
import math
import jax
import jax.numpy as jnp
from jax import lax

D_MODEL = 1024
BATCH = 1
SEQ = 256
DEPTH = 2
DEC_BATCH = 1
DEC_SEQ = 256
PAST_LEN = 128

N_EVEN = (DEPTH + 1) // 2
N_ODD = DEPTH // 2
ALPHA = (2.0 * DEPTH) ** 0.25
BETA = (8.0 * DEPTH) ** -0.25
LN_EPS = 1e-5
D_FF = 2816
CONV_W = 4
CONV_PAD_LEFT = 2
ML_WIDTH = D_MODEL
ML_HEADS = 4
ML_DH = ML_WIDTH // ML_HEADS
ML_QKV_BLOCK = 4
ML_NBLK = ML_WIDTH // ML_QKV_BLOCK
ML_CHUNK = 128
LRU_WIDTH = D_MODEL
LRU_BLOCKS = 16
LRU_BDIM = LRU_WIDTH // LRU_BLOCKS
LRU_C = 8.0
HG_HEADS = 8
HG_DH = 128
HG_WIDTH = HG_HEADS * HG_DH
HG_CHUNK = 16
RET_HEADS = 4
RET_DK = 256
RET_DV = 256
RET_QK_WIDTH = RET_HEADS * RET_DK
RET_WIDTH = RET_HEADS * RET_DV
RET_CHUNK = 128
ROPE_BASE = 10000.0
EVEN_SIZES = [ML_WIDTH, ML_WIDTH, LRU_WIDTH, LRU_WIDTH]
ODD_SIZES = [HG_WIDTH] * 5 + [RET_QK_WIDTH, RET_QK_WIDTH, RET_WIDTH, RET_WIDTH]
EVEN_IN = sum(EVEN_SIZES)
ODD_IN = sum(ODD_SIZES)

kernel_name = 'hybrid_bidir_mlstm_rglru_hgrn2_retnet_encoder'

def _split(h, sizes):
    out, off = [], 0
    for s in sizes:
        out.append(h[..., off:off + s])
        off += s
    return out

def layer_norm(x, g, b):
    xf = x.astype(jnp.float32)
    mu = jnp.mean(xf, axis=-1, keepdims=True)
    var = jnp.mean(jnp.square(xf - mu), axis=-1, keepdims=True)
    return ((xf - mu) * lax.rsqrt(var + LN_EPS) * g + b).astype(x.dtype)

def head_norm(x, g, n_heads, center):
    B, L, W = x.shape
    xf = x.astype(jnp.float32).reshape(B, L, n_heads, W // n_heads)
    if center:
        xf = xf - jnp.mean(xf, axis=-1, keepdims=True)
    xf = xf * lax.rsqrt(jnp.mean(xf * xf, axis=-1, keepdims=True) + LN_EPS)
    return (xf.reshape(B, L, W) * g).astype(x.dtype)

def swiglu_ffn(x, w_in, w_out):
    gate, up = jnp.split(x @ w_in, 2, axis=-1)
    return (jax.nn.silu(gate) * up) @ w_out

def dw_conv(x, w, b):
    C = x.shape[-1]
    y = lax.conv_general_dilated(x, w[:, None, :], window_strides=(1,),
                                 padding=[(CONV_PAD_LEFT, CONV_W - 1 - CONV_PAD_LEFT)],
                                 dimension_numbers=('NWC', 'WIO', 'NWC'), feature_group_count=C)
    return y + b

def _to_chunks(t, chunk):
    B, H, L = t.shape[:3]
    return jnp.moveaxis(t.reshape(B, H, L // chunk, chunk, *t.shape[3:]), 2, 0)

def _from_chunks(t):
    t = jnp.moveaxis(t, 0, 2)
    return t.reshape(t.shape[0], t.shape[1], -1, *t.shape[4:])

def _flip_l(t):
    return jnp.flip(t, axis=2)

def mlstm_chunkwise(q, k, v, log_i, log_f):
    B, H, L, Dk = q.shape
    Dv = v.shape[-1]
    mask = jnp.tril(jnp.ones((ML_CHUNK, ML_CHUNK), dtype=bool))

    def step(carry, inp):
        c_st, n_st, m_st = carry
        qb, kb, vb, ib, fb = inp
        bcum = jnp.cumsum(fb, axis=-1)
        d_log = jnp.where(mask, bcum[..., :, None] - bcum[..., None, :] + ib[..., None, :], -jnp.inf)
        inter_log = bcum + m_st[..., None]
        m_t = jnp.maximum(inter_log, jnp.max(d_log, axis=-1))
        s = jnp.einsum('bhtk,bhsk->bhts', qb, kb) * jnp.exp(d_log - m_t[..., None])
        w_inter = jnp.exp(inter_log - m_t)
        num = jnp.einsum('bhts,bhsv->bhtv', s, vb) + w_inter[..., None] * jnp.einsum('bhtk,bhkv->bhtv', qb, c_st)
        den = jnp.sum(s, axis=-1) + w_inter * jnp.einsum('bhtk,bhk->bht', qb, n_st)
        h = num / jnp.maximum(jnp.abs(den), jnp.exp(-m_t))[..., None]
        b_last = bcum[..., -1]
        g_log = b_last[..., None] - bcum + ib
        m_new = jnp.maximum(b_last + m_st, jnp.max(g_log, axis=-1))
        w_k = jnp.exp(g_log - m_new[..., None])
        decay = jnp.exp(b_last + m_st - m_new)
        c_st = decay[..., None, None] * c_st + jnp.einsum('bhsk,bhsv->bhkv', kb * w_k[..., None], vb)
        n_st = decay[..., None] * n_st + jnp.einsum('bhsk,bhs->bhk', kb, w_k)
        return (c_st, n_st, m_new), h

    init = (jnp.zeros((B, H, Dk, Dv), jnp.float32), jnp.zeros((B, H, Dk), jnp.float32),
            jnp.zeros((B, H), jnp.float32))
    xs = tuple(_to_chunks(t, ML_CHUNK) for t in (q, k, v, log_i, log_f))
    _, h = lax.scan(step, init, xs)
    return _from_chunks(h)

def mlstm_mixer(u, z, conv_w, conv_b, wq, wk, wv, w_ig, b_ig, w_fg, b_fg, norm_g):
    B, L, _ = u.shape
    c = jax.nn.silu(dw_conv(u, conv_w, conv_b))

    def blockdiag(t, w):
        return jnp.einsum('blnc,ncd->blnd', t.reshape(B, L, ML_NBLK, ML_QKV_BLOCK), w).reshape(B, L, ML_WIDTH)

    q = blockdiag(c, wq)
    k = blockdiag(c, wk) / math.sqrt(ML_DH)
    v = blockdiag(u, wv)
    qkv = jnp.concatenate([q, k, v], axis=-1)
    i_pre = jnp.einsum('bld,rdh->rbhl', qkv, w_ig).astype(jnp.float32) + b_ig[:, None, :, None]
    log_f = jax.nn.log_sigmoid(jnp.einsum('bld,rdh->rbhl', qkv, w_fg).astype(jnp.float32) + b_fg[:, None, :, None])

    def heads(t):
        return t.reshape(B, L, ML_HEADS, ML_DH).transpose(0, 2, 1, 3).astype(jnp.float32)

    qh, kh, vh = heads(q), heads(k), heads(v)
    h_f = mlstm_chunkwise(qh, kh, vh, i_pre[0], log_f[0])
    h_b = _flip_l(mlstm_chunkwise(_flip_l(qh), _flip_l(kh), _flip_l(vh), _flip_l(i_pre[1]), _flip_l(log_f[1])))
    h = (h_f + h_b).transpose(0, 2, 1, 3).reshape(B, L, ML_WIDTH).astype(u.dtype)
    return jax.nn.sigmoid(z) * head_norm(h, norm_g, ML_HEADS, True)

def _linear_combine(e1, e2):
    a1, b1 = e1
    a2, b2 = e2
    return a1 * a2, a2 * b1 + b2

def rglru_direction(x, w_a, b_a, w_x, b_x, lam):
    B, L, W = x.shape
    xb = x.reshape(B, L, LRU_BLOCKS, LRU_BDIM)
    r = jax.nn.sigmoid((jnp.einsum('blnc,ncd->blnd', xb, w_a).reshape(B, L, W) + b_a).astype(jnp.float32))
    i = jax.nn.sigmoid((jnp.einsum('blnc,ncd->blnd', xb, w_x).reshape(B, L, W) + b_x).astype(jnp.float32))
    log_a = -LRU_C * r * jax.nn.softplus(-lam.astype(jnp.float32))
    a = jnp.exp(log_a)
    b = jnp.sqrt(-jnp.expm1(2.0 * log_a)) * i * x.astype(jnp.float32)
    _, h = lax.associative_scan(_linear_combine, (a, b), axis=1)
    return h

def rglru_mixer(u, g, conv_w, conv_b, w_a, b_a, w_x, b_x, lam):
    x = dw_conv(u, conv_w, conv_b)
    h_f = rglru_direction(x, w_a[0], b_a[0], w_x[0], b_x[0], lam[0])
    h_b = jnp.flip(rglru_direction(jnp.flip(x, 1), w_a[1], b_a[1], w_x[1], b_x[1], lam[1]), 1)
    return (h_f + h_b).astype(u.dtype) * jax.nn.gelu(g)

def gla_chunkwise(q, k, v, log_g):
    B, H, L, K = q.shape
    V = v.shape[-1]
    mask = jnp.tril(jnp.ones((HG_CHUNK, HG_CHUNK), dtype=bool))[:, :, None]

    def step(s_st, inp):
        qb, kb, vb, gb = inp
        bc = jnp.cumsum(gb, axis=2)
        diff = bc[:, :, :, None, :] - bc[:, :, None, :, :]
        wdec = jnp.exp(jnp.where(mask, diff, -jnp.inf))
        att = jnp.einsum('bhtk,bhtsk,bhsk->bhts', qb, wdec, kb)
        o = jnp.einsum('bhts,bhsv->bhtv', att, vb) + jnp.einsum('bhtk,bhkv->bhtv', qb * jnp.exp(bc), s_st)
        b_last = bc[:, :, -1]
        s_st = jnp.exp(b_last)[..., None] * s_st + jnp.einsum('bhsk,bhsv->bhkv', kb * jnp.exp(b_last[:, :, None] - bc), vb)
        return s_st, o

    init = jnp.zeros((B, H, K, V), jnp.float32)
    xs = tuple(_to_chunks(t, HG_CHUNK) for t in (q, k, v, log_g))
    _, o = lax.scan(step, init, xs)
    return _from_chunks(o)

def hgrn2_mixer(q, f_fwd, f_bwd, i, g, lb, norm_g):
    B, L, _ = q.shape

    def heads(t):
        return t.reshape(B, L, HG_HEADS, -1).transpose(0, 2, 1, 3).astype(jnp.float32)

    qh = heads(jax.nn.silu(q))
    vh = heads(i)
    f_f = lb + (1.0 - lb) * jax.nn.sigmoid(f_fwd.astype(jnp.float32))
    f_b = lb + (1.0 - lb) * jax.nn.sigmoid(f_bwd.astype(jnp.float32))
    o_f = gla_chunkwise(qh, heads(1.0 - f_f), vh, heads(jnp.log(f_f)))
    o_b = _flip_l(gla_chunkwise(_flip_l(qh), _flip_l(heads(1.0 - f_b)), _flip_l(vh), _flip_l(heads(jnp.log(f_b)))))
    o = (o_f + o_b).transpose(0, 2, 1, 3).reshape(B, L, HG_WIDTH).astype(q.dtype)
    return head_norm(o, norm_g, HG_HEADS, False) * jax.nn.silu(g)

def _retention_log_gammas():
    lg = jnp.log(1.0 - 2.0 ** (-5.0 - jnp.arange(RET_HEADS, dtype=jnp.float32)))
    return lg, lg[::-1]

def rope_tables(L):
    pos = jnp.arange(L, dtype=jnp.float32)
    inv = ROPE_BASE ** (-jnp.arange(RET_DK // 2, dtype=jnp.float32) / (RET_DK // 2))
    ang = pos[:, None] * inv[None, :]
    return jnp.cos(ang), jnp.sin(ang)

def apply_rope(t, cos, sin):
    half = t.shape[-1] // 2
    t1, t2 = t[..., :half], t[..., half:]
    return jnp.concatenate([t1 * cos - t2 * sin, t1 * sin + t2 * cos], axis=-1)

def retention_chunkwise(q, k, v, log_gamma):
    B, H, L, K = q.shape
    V = v.shape[-1]
    pos = jnp.arange(RET_CHUNK, dtype=jnp.float32)
    diff = pos[:, None] - pos[None, :]
    intra = jnp.exp(jnp.where(diff >= 0, diff[None] * log_gamma[:, None, None], -jnp.inf))
    q_scale = jnp.exp((pos[None, :] + 1.0) * log_gamma[:, None])
    k_scale = jnp.exp((RET_CHUNK - 1.0 - pos[None, :]) * log_gamma[:, None])
    chunk_decay = jnp.exp(RET_CHUNK * log_gamma)

    def step(r_st, inp):
        qb, kb, vb = inp
        att = jnp.einsum('bhtk,bhsk->bhts', qb, kb) * intra
        o = jnp.einsum('bhts,bhsv->bhtv', att, vb) + q_scale[..., None] * jnp.einsum('bhtk,bhkv->bhtv', qb, r_st)
        r_st = chunk_decay[:, None, None] * r_st + jnp.einsum('bhsk,bhsv->bhkv', kb * k_scale[..., None], vb)
        return r_st, o

    init = jnp.zeros((B, H, K, V), jnp.float32)
    xs = tuple(_to_chunks(t, RET_CHUNK) for t in (q, k, v))
    _, o = lax.scan(step, init, xs)
    return _from_chunks(o)

def retention_mixer(q, k, v, g, cos, sin, norm_g):
    B, L, _ = q.shape

    def heads(t):
        return t.reshape(B, L, RET_HEADS, -1).transpose(0, 2, 1, 3).astype(jnp.float32)

    qh = apply_rope(heads(q), cos, sin)
    kh = apply_rope(heads(k), cos, sin) / math.sqrt(RET_DK)
    vh = heads(v)
    lg_f, lg_b = _retention_log_gammas()
    o_f = retention_chunkwise(qh, kh, vh, lg_f)
    o_b = _flip_l(retention_chunkwise(_flip_l(qh), _flip_l(kh), _flip_l(vh), lg_b))
    o = (o_f + o_b).transpose(0, 2, 1, 3).reshape(B, L, RET_WIDTH).astype(q.dtype)
    return head_norm(o, norm_g, RET_HEADS, True) * jax.nn.silu(g)

def even_mixer(x, w_in, w_out, ml_conv_w, ml_conv_b, ml_wq, ml_wk, ml_wv, ml_w_ig, ml_b_ig,
               ml_w_fg, ml_b_fg, ml_norm_g, lru_conv_w, lru_conv_b, lru_w_a, lru_b_a, lru_w_x,
               lru_b_x, lru_lambda):
    u_m, z_m, u_r, g_r = _split(x @ w_in, EVEN_SIZES)
    y_m = mlstm_mixer(u_m, z_m, ml_conv_w, ml_conv_b, ml_wq, ml_wk, ml_wv, ml_w_ig, ml_b_ig,
                      ml_w_fg, ml_b_fg, ml_norm_g)
    y_r = rglru_mixer(u_r, g_r, lru_conv_w, lru_conv_b, lru_w_a, lru_b_a, lru_w_x, lru_b_x, lru_lambda)
    return jnp.concatenate([y_m, y_r], axis=-1) @ w_out

def odd_mixer(x, w_in, w_out, lb, hg_norm_g, ret_norm_g, cos, sin):
    q_c, f_f, f_b, i_c, g_c, q_r, k_r, v_r, g_r = _split(x @ w_in, ODD_SIZES)
    y_c = hgrn2_mixer(q_c, f_f, f_b, i_c, g_c, lb, hg_norm_g)
    y_r = retention_mixer(q_r, k_r, v_r, g_r, cos, sin, ret_norm_g)
    return jnp.concatenate([y_c, y_r], axis=-1) @ w_out

def setup_inputs(seed: int = 0) -> dict:
    key = jax.random.key(seed)
    ks = iter(jax.random.split(key, 48))
    f32 = jnp.float32

    def nrm(shape, scale):
        return jax.random.normal(next(ks), shape, f32) * scale

    x_prompt = nrm((BATCH, SEQ, D_MODEL), 1.0)
    x_sample = nrm((DEC_BATCH, DEC_SEQ, D_MODEL), 1.0)
    ffn_a_w_in = nrm((DEPTH, D_MODEL, 2 * D_FF), D_MODEL ** -0.5)
    ffn_a_w_out = nrm((DEPTH, D_FF, D_MODEL), BETA * D_FF ** -0.5)
    ffn_b_w_in = nrm((DEPTH, D_MODEL, 2 * D_FF), D_MODEL ** -0.5)
    ffn_b_w_out = nrm((DEPTH, D_FF, D_MODEL), BETA * D_FF ** -0.5)
    ln_g = 1.0 + nrm((DEPTH, 3, D_MODEL), 0.05)
    ln_b = nrm((DEPTH, 3, D_MODEL), 0.01)
    ev_w_in = nrm((N_EVEN, D_MODEL, EVEN_IN), D_MODEL ** -0.5)
    ev_w_out = nrm((N_EVEN, ML_WIDTH + LRU_WIDTH, D_MODEL), BETA * (ML_WIDTH + LRU_WIDTH) ** -0.5)
    ml_conv_w = nrm((N_EVEN, CONV_W, ML_WIDTH), CONV_W ** -0.5)
    ml_conv_b = nrm((N_EVEN, ML_WIDTH), 0.01)
    ml_wq = nrm((N_EVEN, ML_NBLK, ML_QKV_BLOCK, ML_QKV_BLOCK), ML_QKV_BLOCK ** -0.5)
    ml_wk = nrm((N_EVEN, ML_NBLK, ML_QKV_BLOCK, ML_QKV_BLOCK), ML_QKV_BLOCK ** -0.5)
    ml_wv = nrm((N_EVEN, ML_NBLK, ML_QKV_BLOCK, ML_QKV_BLOCK), ML_QKV_BLOCK ** -0.5)
    ml_w_ig = nrm((N_EVEN, 2, 3 * ML_WIDTH, ML_HEADS), 0.1 * (3 * ML_WIDTH) ** -0.5)
    ml_b_ig = nrm((N_EVEN, 2, ML_HEADS), 0.1)
    ml_w_fg = nrm((N_EVEN, 2, 3 * ML_WIDTH, ML_HEADS), 0.1 * (3 * ML_WIDTH) ** -0.5)
    ml_b_fg = jnp.linspace(3.0, 6.0, ML_HEADS, dtype=f32) + nrm((N_EVEN, 2, ML_HEADS), 0.1)
    ml_norm_g = 1.0 + nrm((N_EVEN, ML_WIDTH), 0.05)
    lru_conv_w = nrm((N_EVEN, CONV_W, LRU_WIDTH), CONV_W ** -0.5)
    lru_conv_b = nrm((N_EVEN, LRU_WIDTH), 0.01)
    lru_w_a = nrm((N_EVEN, 2, LRU_BLOCKS, LRU_BDIM, LRU_BDIM), LRU_BDIM ** -0.5)
    lru_b_a = nrm((N_EVEN, 2, LRU_WIDTH), 0.01)
    lru_w_x = nrm((N_EVEN, 2, LRU_BLOCKS, LRU_BDIM, LRU_BDIM), LRU_BDIM ** -0.5)
    lru_b_x = nrm((N_EVEN, 2, LRU_WIDTH), 0.01)
    a0 = jax.random.uniform(next(ks), (N_EVEN, 2, LRU_WIDTH), f32, 0.9, 0.999)
    p = a0 ** (1.0 / LRU_C)
    lru_lambda = jnp.log(p) - jnp.log1p(-p)
    od_w_in = nrm((N_ODD, D_MODEL, ODD_IN), D_MODEL ** -0.5)
    od_w_out = nrm((N_ODD, HG_WIDTH + RET_WIDTH, D_MODEL), BETA * (HG_WIDTH + RET_WIDTH) ** -0.5)
    hg_lb_logits = nrm((DEPTH, HG_WIDTH), 0.1)
    hg_norm_g = 1.0 + nrm((N_ODD, HG_WIDTH), 0.05)
    ret_norm_g = 1.0 + nrm((N_ODD, RET_WIDTH), 0.05)
    return {'x_prompt': x_prompt, 'x_sample': x_sample,
            'ffn_a_w_in': ffn_a_w_in, 'ffn_a_w_out': ffn_a_w_out,
            'ffn_b_w_in': ffn_b_w_in, 'ffn_b_w_out': ffn_b_w_out,
            'ln_g': ln_g, 'ln_b': ln_b,
            'ev_w_in': ev_w_in, 'ev_w_out': ev_w_out,
            'ml_conv_w': ml_conv_w, 'ml_conv_b': ml_conv_b,
            'ml_wq': ml_wq, 'ml_wk': ml_wk, 'ml_wv': ml_wv,
            'ml_w_ig': ml_w_ig, 'ml_b_ig': ml_b_ig, 'ml_w_fg': ml_w_fg, 'ml_b_fg': ml_b_fg,
            'ml_norm_g': ml_norm_g,
            'lru_conv_w': lru_conv_w, 'lru_conv_b': lru_conv_b,
            'lru_w_a': lru_w_a, 'lru_b_a': lru_b_a, 'lru_w_x': lru_w_x, 'lru_b_x': lru_b_x,
            'lru_lambda': lru_lambda,
            'od_w_in': od_w_in, 'od_w_out': od_w_out,
            'hg_lb_logits': hg_lb_logits, 'hg_norm_g': hg_norm_g, 'ret_norm_g': ret_norm_g}

def reference(x_prompt, x_sample, ffn_a_w_in, ffn_a_w_out, ffn_b_w_in, ffn_b_w_out, ln_g, ln_b,
              ev_w_in, ev_w_out, ml_conv_w, ml_conv_b, ml_wq, ml_wk, ml_wv, ml_w_ig, ml_b_ig,
              ml_w_fg, ml_b_fg, ml_norm_g, lru_conv_w, lru_conv_b, lru_w_a, lru_b_a, lru_w_x,
              lru_b_x, lru_lambda, od_w_in, od_w_out, hg_lb_logits, hg_norm_g, ret_norm_g):
    lbs = jnp.cumsum(jax.nn.softmax(hg_lb_logits.astype(jnp.float32), axis=0), axis=0)
    lbs = lbs - lbs[0]

    def trunk(x):
        cos, sin = rope_tables(x.shape[1])
        for l in range(DEPTH):
            x = layer_norm(ALPHA * x + 0.5 * swiglu_ffn(x, ffn_a_w_in[l], ffn_a_w_out[l]), ln_g[l, 0], ln_b[l, 0])
            if l % 2 == 0:
                e = l // 2
                mix = even_mixer(x, ev_w_in[e], ev_w_out[e], ml_conv_w[e], ml_conv_b[e], ml_wq[e], ml_wk[e],
                                 ml_wv[e], ml_w_ig[e], ml_b_ig[e], ml_w_fg[e], ml_b_fg[e], ml_norm_g[e],
                                 lru_conv_w[e], lru_conv_b[e], lru_w_a[e], lru_b_a[e], lru_w_x[e],
                                 lru_b_x[e], lru_lambda[e])
            else:
                o = l // 2
                mix = odd_mixer(x, od_w_in[o], od_w_out[o], lbs[l], hg_norm_g[o], ret_norm_g[o], cos, sin)
            x = layer_norm(ALPHA * x + mix, ln_g[l, 1], ln_b[l, 1])
            x = layer_norm(ALPHA * x + 0.5 * swiglu_ffn(x, ffn_b_w_in[l], ffn_b_w_out[l]), ln_g[l, 2], ln_b[l, 2])
        return x

    y_prompt = trunk(x_prompt)
    y_sample = trunk(x_sample)
    return (y_prompt, y_sample)


_drawn_inputs = setup_inputs


def setup_inputs(seed=0):
    import zlib

    import numpy as np

    out = dict(_drawn_inputs(seed))
    spreads = {}
    factors = {'ml_conv_b': 8.0,
     'ml_w_ig': 6.305,
     'ml_b_ig': 8.0,
     'ml_w_fg': 8.0,
     'ml_norm_g': 8.0,
     'lru_conv_b': 4.332,
     'lru_b_a': 174.543,
     'lru_b_x': 64.0,
     'hg_lb_logits': 8.0,
     'hg_norm_g': 7.496,
     'ret_norm_g': 7.898}
    for name, (base, spread) in spreads.items():
        noise = np.random.default_rng([zlib.crc32(name.encode()), seed]).standard_normal(out[name].shape)
        drawn = base * np.exp(spread * noise) if base else spread * noise
        out[name] = jnp.asarray(drawn.astype(out[name].dtype))
    for name, factor in factors.items():
        out[name] = (out[name] * factor).astype(out[name].dtype)
    return out
```

```python
from contextlib import ExitStack

import concourse.bass as bass
import numpy as np
from concourse import mybir

F32 = mybir.dt.float32
F32R = mybir.dt.float32r
U8 = mybir.dt.uint8
ALU = mybir.AluOpType
ACT = mybir.ActivationFunctionType

P = 128
SEQS, L = 2, 256
T = SEQS * L
SB = L // P
NB = SEQS * SB
D = 1024
KD = D // P
FF = 2816
FT = FF // P
KH = FT // 2
DEPTH = 2
ALPHA = (2.0 * DEPTH) ** 0.25
EPS = 1e-5
IN_SLOTS, OUT_SLOTS = 2 * FT, 2 * KD
EV_SLOTS, OD_SLOTS = 4 * KD, 9 * KD
NH = 4
HT = 2
HG = 8
LEVELS = 7
PAD = 3
AHEAD = (1, 3, 4, 5)

VEC = {}
for _name, _n in (("ln_g", 6 * KD), ("ln_b", 6 * KD), ("ml_cw", 4 * KD), ("ml_cb", KD), ("ml_g", KD),
                  ("lru_cw", 4 * KD), ("lru_cb", KD), ("b_a", 2 * KD), ("b_x", 2 * KD), ("lam", 2 * KD),
                  ("lb", 2 * KD), ("hg_g", KD), ("ret_g", KD)):
    VEC[_name] = sum(n for _, n in VEC.values()), _n
NV = sum(n for _, n in VEC.values())
CON = {}
for _name, _n in (("ident", P), ("mean_d", P), ("mean_256", P), ("mean_128", P), ("ones", P), ("zeros", P),
                  ("tri", 2 * L), ("bd", 32)):
    CON[_name] = sum(n for _, n in CON.values()), _n
NC = sum(n for _, n in CON.values())
NO = 2 * L + NH * 3 * P


def build(nc, a):
    off = [(nc.sbuf_base + 63) // 64 * 64]

    def at(name, shape, dt, where):
        return nc.alloc_sbuf_tensor_at(name, shape, dt, offset=where)

    def size(shape, dt):
        n = 1
        for s in shape[1:]:
            n *= s
        return (n * (1 if dt == U8 else 4) + 31) // 32 * 32

    def sb(name, shape, dt=F32, area=off):
        t = at("sb_" + name, shape, dt, area[0])
        area[0] += size(shape, dt)
        assert area[0] <= nc.sbuf_usable_end, (name, area[0], nc.sbuf_usable_end)
        return t

    x = sb("x", [P, KD, T])
    xh = sb("xh", [P, KD, T], F32R)
    xl = sb("xl", [P, KD, T], F32R)
    raw = sb("raw", [P, 2, KH * P])
    wh = sb("wh", [P, 2, KH * P], F32R)
    wl = sb("wl", [P, 2, KH * P], F32R)
    con = sb("con", [P, NC])
    vec = sb("vec", [P, NV])
    pmask = sb("pmask", [P, LEVELS, P], U8)
    w4 = sb("w4", [P, 3, KD, 4])
    wg = sb("wg", [P, 3 * KD, 4, NH])
    gb = sb("gb", [NH, 4])
    sel = sb("sel", [NH, NH, P])
    sp = sb("sp", [P, 3, 2 * KD])
    hbias = sb("hbias", [P, 4 * KD])
    lb = sb("lb", [P, 3, KD])
    gT = sb("gT", [P, 2, NB, NH])
    odd_area = [off[0]]
    odc = sb("odc", [P, NO], F32, odd_area)
    ev_area = [off[0]]
    negM = sb("negM", [NH, 2, T], F32, ev_area)
    thr = sb("thr", [NH, 2, T], F32, ev_area)
    free = max(odd_area[0], ev_area[0])

    fa = [free]
    hh = sb("hh", [P, FT, T], F32R, fa)
    hl = sb("hl", [P, FT, T], F32R, fa)
    sg = sb("sg", [P, 2, T], F32, fa)
    hf = sb("hf", [P, 2, T], F32, fa)
    sq = at("sb_sq", [P, KD, T], F32, free)
    mask_f = at("sb_mask_f", [P, LEVELS, P], F32, fa[0] - LEVELS * P * 4)
    ma = [free]
    yhA = sb("yhA", [P, KD, T], F32R, ma)
    ylA = sb("ylA", [P, KD, T], F32R, ma)
    yB = ma[0]
    yhB = sb("yhB", [P, KD, T], F32R, ma)
    ylB = sb("ylB", [P, KD, T], F32R, ma)
    qk_area = [yB]
    q_all = sb("q_all", [P, KD, T], F32, qk_area)
    k_all = sb("k_all", [P, KD, T], F32, qk_area)
    tmp = ma[0]
    va = [tmp]
    vT = sb("vT", [P, NB, D], F32, va)
    e1 = [va[0]]
    um = sb("um", [P, 2, SEQS, L + PAD + 1], F32, e1)
    cv = sb("cv", [P, SEQS, L], F32, e1)
    cc = sb("cc", [P, 2, T], F32, e1)
    vf = sb("vf", [P, 2, T], F32, e1)
    bd = sb("bd", [P, 3, P], F32, e1)
    gtok = sb("gtok", [P, NB, 4, NH], F32, e1)
    e2 = [va[0]]
    gi = sb("gi", [NH, 2, T], F32, e2)
    gf = sb("gf", [NH, 2, T], F32, e2)
    g1 = sb("g1", [NH, 2, T], F32, e2)
    g2 = sb("g2", [NH, 2, T], F32, e2)
    one = sb("one", [NH, L], F32, e2)
    e3 = [va[0]]
    Ef = sb("Ef", [P, SEQS, L + P], F32, e3)
    Eb = sb("Eb", [P, SEQS, L + P], F32, e3)
    att = sb("att", [P, SEQS, SB, L], F32, e3)
    rec = sb("rec", [P, 2, T], F32, e3)
    hv = sb("hv", [P, HT, T], F32, e3)
    zs = sb("zs", [P, HT, T], F32, e3)
    dab = sb("dab", [P, T], F32, e3)
    rs = sb("rs", [P, T], F32, e3)
    ea = [tmp]
    lbd = sb("lbd", [P, 2, 4, P], F32, ea)
    lum = sb("lum", [P, SEQS, L + PAD + 1], F32, ea)
    lx = sb("lx", [P, SEQS, L], F32, ea)
    th = sb("th", [P, 2, 2, T], F32, ea)
    la = sb("la", [P, 2, T], F32, ea)
    lw = sb("lw", [P, 2, T], F32, ea)
    lr = sb("lr", [P, 2, T], F32, ea)
    lq = sb("lq", [P, 2, T], F32, ea)
    lix = sb("lix", [P, 2, T], F32, ea)
    lgl = sb("lgl", [P, T], F32, ea)
    ha = [tmp]
    hq = sb("hq", [P, T], F32, ha)
    TA = sb("TA", [P, 3, T], F32, ha)
    TB = sb("TB", [P, 3, T // 2], F32, ha)
    Lo = sb("Lo", [P, 2, T], F32, ha)
    Up = sb("Up", [P, 2, T], F32, ha)
    KQ = sb("KQ", [P, 2, T], F32, ha)
    ks = sb("ks", [P, T], F32, ha)
    hat = sb("hat", [P, 2, NB, P], F32, ha)
    hi_ = sb("hi_", [P, T], F32, ha)
    hvt = sb("hvt", [P, NB, P], F32, ha)
    hgs = sb("hgs", [P, T], F32, ha)
    ho = sb("ho", [P, T], F32, ha)
    hsq = sb("hsq", [P, T], F32, ha)
    hrs = sb("hrs", [P, T], F32, ha)
    ra = [tmp]
    rq = sb("rq", [P, HT, T], F32, ra)
    rk = sb("rk", [P, HT, T], F32, ra)
    rt = sb("rt", [P, 4, T], F32, ra)
    rv = sb("rv", [P, T], F32, ra)
    rvt = sb("rvt", [P, NB, HT, P], F32, ra)
    ratt = sb("ratt", [P, SEQS, SB, L], F32, ra)
    rhv = sb("rhv", [P, HT, T], F32, ra)
    rzs = sb("rzs", [P, HT, T], F32, ra)
    rrec = sb("rrec", [P, T], F32, ra)

    def cn(name):
        o, n = CON[name]
        return con[:, o:o + n]

    def vc(name, i, n=1):
        return vec[:, bass.ds(VEC[name][0] + i, n)]

    ident, tri = cn("ident"), cn("tri")
    cos, sin = odc[:, 0:L], odc[:, L:2 * L]

    def seqs(ap):
        return ap.rearrange("p (s t) -> p s t", s=SEQS)

    def blocks(ap):
        return ap.rearrange("p (b t) -> p b t", b=NB)

    def halves(ap, B):
        v = ap.rearrange("p r (n two b) -> p r n two b", two=2, b=B)
        return v[:, :, :, 0, :], v[:, :, :, 1, :]

    def spread(ap, B):
        return ap[:, :, :, None].to_broadcast([P, 2, T // (2 * B), B])

    with ExitStack() as ctx:
        ps = ctx.enter_context(nc.psum_tensor("ps", [P, 8, T], F32))

        def sem(name):
            return ctx.enter_context(nc.semaphore("s_" + name))

        const_in, odd_in, x_in, out_done = sem("const_in"), sem("odd_in"), sem("x_in"), sem("out_done")
        raw_in, bd_in = [sem("raw_in0"), sem("raw_in1")], [sem("bd_in0"), sem("bd_in1")]
        hi_done, lo_done, w_used = sem("hi_done"), sem("lo_done"), sem("w_used")
        prep_d, prep_a = sem("prep_d"), sem("prep_a")
        step_done = sem("step_done")
        y_done, mean_mm, cen_done, sq_done = sem("y_done"), sem("mean_mm"), sem("cen_done"), sem("sq_done")
        var_mm, var_in, rstd_done = sem("var_mm"), sem("var_in"), sem("rstd_done")
        x_done, xh_done, xl_done = sem("x_done"), sem("xh_done"), sem("xl_done")
        silu_done, glu_done, h_done = sem("silu_done"), sem("glu_done"), sem("h_done")
        um_zero, u_ev, c_lin, c_done, bd_done = sem("um_zero"), sem("u_ev"), sem("c_lin"), sem("c_done"), sem("bd_done")
        q_mm, k_mm, v_mm, q_ev, k_ev, v_ev = (sem(n) for n in ("q_mm", "k_mm", "v_mm", "q_ev", "k_ev", "v_ev"))
        vt_mm, vt_ev, gates_mm, gtok_ev, rows_mm = (sem(n) for n in ("vt_mm", "vt_ev", "gates_mm", "gtok_ev", "rows_mm"))
        rows_a, g_done, marg_done, thr_done, gT_mm, gT_ev = (
            sem(n) for n in ("rows_a", "g_done", "marg_done", "thr_done", "gT_mm", "gT_ev"))
        mb_mm, tb_mm, tb_ev, qk_mm, t_done, e_done, s_done = (
            sem(n) for n in ("mb_mm", "tb_mm", "tb_ev", "qk_mm", "t_done", "e_done", "s_done"))
        den_mm, abs_done, dmax_done, att_done, z_done = (
            sem(n) for n in ("den_mm", "abs_done", "dmax_done", "att_done", "z_done"))
        pv_mm, hv_done, hmean_mm, hcen_done, hsq_done = (
            sem(n) for n in ("pv_mm", "hv_done", "hmean_mm", "hcen_done", "hsq_done"))
        hvar_mm, hvar_in, hrstd_done = sem("hvar_mm"), sem("hvar_in"), sem("hrstd_done")
        mix_done = sem("mix_done")
        lzero, lu_ev, lx_done, lg_mm, gelu_done, lt_done = (
            sem(n) for n in ("lzero", "lu_ev", "lx_done", "lg_mm", "gelu_done", "lt_done"))
        la_done, lw_done, lq_done, lsq_done, lix_done = (
            sem(n) for n in ("la_done", "lw_done", "lq_done", "lsq_done", "lix_done"))
        a_sig, a_i, a_q, a_kq, a_g, a_vt_mm, a_vt = (
            sem(n) for n in ("a_sig", "a_i", "a_q", "a_kq", "a_g", "a_vt_mm", "a_vt"))
        a_diag_mm, a_diag, a_cp, a_lv_mm, a_up, a_pred = (
            sem(n) for n in ("a_diag_mm", "a_diag", "a_cp", "a_lv_mm", "a_up", "a_pred"))
        a_off_mm, a_off, a_pv, a_sq, a_var, a_vin, a_rstd = (
            sem(n) for n in ("a_off_mm", "a_off", "a_pv", "a_sq", "a_var", "a_vin", "a_rstd"))
        r_q, r_k, rv_ev, rvt_mm, rvt_ev, rqk_mm, ratt_done, rz_ev, rz_done = (
            sem(n) for n in ("r_q", "r_k", "rv_ev", "rvt_mm", "rvt_ev", "rqk_mm", "ratt_done", "rz_ev", "rz_done"))

        kinds = ["ffn", "even", "ffn", "ffn", "odd", "ffn"]
        own = {"ffn": IN_SLOTS, "even": EV_SLOTS, "odd": OD_SLOTS}
        stages = []
        for kind in kinds:
            n0 = sum(own[k] + OUT_SLOTS for k, _, _ in stages)
            stages.append((kind, n0, sum(k == "ffn" for k, _, _ in stages)))
        MIX_EVEN, MIX_ODD = NH + KD, HG + NH

        class Slot:

            def __init__(self, n0, i, per, j):
                self.half, self.par = n0 // 2 + (per // 2) * i + j // 2, j % 2
                self.n = 2 * self.half + self.par

        block = ctx.enter_context(nc.Block())

        @block.sync
        def _(sync):
            def load(src, kt, sl):
                sync.wait_ge(hi_done, sl.n + 1)
                sync.wait_ge(lo_done, sl.n + 1)
                sync.dma_start(raw[:, sl.par, 0:kt * P], src).then_inc(raw_in[sl.par], 16)

            def stream(w, first, n, kt, n0):
                with sync.Fori(0, n // 2) as i:
                    for j in range(2):
                        load(slot_of(w, first + 2 * i + j), kt, Slot(n0, i, 2, j))

            def slot_of(w, n):
                return w[bass.ds(n, 1), :, :].rearrange("a p c -> (a p) c")

            sync.dma_start(x[:], a["x_in"].rearrange("k p t -> p k t")).then_inc(x_in, 16)
            for kind, n0, fi in stages:
                if kind == "ffn":
                    stream(a["w_in"], fi * IN_SLOTS, IN_SLOTS, KD, n0)
                    stream(a["w_out"], fi * OUT_SLOTS, OUT_SLOTS, KH, n0 + IN_SLOTS)
                elif kind == "even":
                    stream(a["w_ev"], 0, 2 * KD, KD, n0)
                    with sync.Fori(0, KD // 2) as i:
                        for j in range(2):
                            for h in range(2):
                                load(slot_of(a["w_ev"], 2 * KD + 4 * i + 2 * j + h), KD,
                                     Slot(n0 + 2 * KD, i, 4, 2 * j + h))
                            sync.wait_ge(lzero, 1)
                            sync.wait_ge(lg_mm, 8 * i + 1)
                            for b in range(2):
                                sync.dma_start(
                                    lbd[64 * b:64 * b + 64, j, :, 64 * b:64 * b + 64],
                                    a["w_lru"][bass.ds(4 * i + 2 * j + b, 1), :, :, :].rearrange(
                                        "a c g d -> (a c) g d")).then_inc(bd_in[j], 16)
                    stream(a["w_evo"], 0, OUT_SLOTS, KD, n0 + EV_SLOTS)
                else:
                    sync.wait_ge(mix_done, MIX_EVEN)
                    sync.dma_start(odc[:], a["odc"]).then_inc(odd_in, 16)
                    stream(a["w_od"], 0, OD_SLOTS, KD, n0)
                    stream(a["w_odo"], 0, OUT_SLOTS, KD, n0 + OD_SLOTS)
            sync.wait_ge(x_done, KD * len(stages))
            sync.dma_start(a["out"].rearrange("k p t -> p k t"), x[:]).then_inc(out_done, 16)
            sync.wait_ge(out_done, 16)

        @block.gpsimd
        def _(pool):
            pool.sem_inc(lo_done, 2)
            pool.sem_inc(lix_done, 1)
            for t, name in ((con, "con"), (vec, "vec"), (mask_f, "pmask"), (w4, "w4"), (wg, "wg"), (gb, "gb"), (sel, "sel")):
                pool.dma_start(t[:], a[name]).then_inc(const_in, 16)

            def lo(kt, sl):
                pool.wait_ge(hi_done, sl.n + 3)
                n = kt * P
                pool.tensor_tensor(wl[:, sl.par, 0:n], raw[:, sl.par, 0:n], wh[:, sl.par, 0:n].bitcast(F32),
                                   ALU.subtract).then_inc(lo_done, 1)

            def los(n, kt, n0):
                with pool.Fori(0, n // 2) as i:
                    for j in range(2):
                        lo(kt, Slot(n0, i, 2, j))

            for kind, n0, fi in stages:
                if kind == "ffn":
                    los(IN_SLOTS, KD, n0)
                    los(OUT_SLOTS, KH, n0 + IN_SLOTS)
                elif kind == "even":
                    los(2 * KD, KD, n0)
                    with pool.Fori(0, KD) as t:
                        for j in range(2):
                            lo(KD, Slot(n0 + 2 * KD, t, 2, j))
                        pool.wait_ge(lt_done, 4 * t + 5)
                        pool.wait_ge(mix_done, NH + t)
                        x_ = lx[:].rearrange("p s t -> p (s t)")[:, None, :].to_broadcast([P, 2, T])
                        pool.tensor_tensor(lix[:], th[:, 1, :, :], x_, ALU.mult).then_inc(lix_done, 1)
                        pool.wait_ge(lix_done, 2 * t + 2)
                        pool.tensor_tensor(lix[:], lix[:], x_, ALU.add).then_inc(lix_done, 1)
                    los(OUT_SLOTS, KD, n0 + EV_SLOTS)
                else:
                    los(OD_SLOTS, KD, n0)
                    los(OUT_SLOTS, KD, n0 + OD_SLOTS)

        @block.tensor
        def _(pe):
            pe.sem_inc(w_used, 2)
            for s in (lg_mm, rvt_mm, a_pv):
                pe.sem_inc(s, 1)

            def proj(bank, kt, sl, rh, rl, start=True, stop=True):
                pe.wait_ge(hi_done, sl.n + 3)
                pe.wait_ge(lo_done, sl.n + 3)
                out = ps[:, bank, :]
                for k in range(kt):
                    w_h, w_l = (w[:, sl.par, k * P:k * P + P] for w in (wh, wl))
                    pe.matmul(out, w_l, rh(k), start=start and k == 0, stop=False)
                    pe.matmul(out, w_h, rl(k), start=False, stop=False)
                    mm = pe.matmul(out, w_h, rh(k), start=False, stop=stop and k == kt - 1)
                mm.then_inc(w_used, 1)

            def of_x(bank, sl):
                proj(bank, KD, sl, lambda k: xh[:, k, :], lambda k: xl[:, k, :])

            def ffn_in(fi, n0):
                with pe.Fori(0, FT // 2) as i:
                    for b in range(2):
                        pe.wait_ge(glu_done, FT * fi + 2 * i + b + 1)
                        of_x(2 * b, Slot(n0, i, 4, 2 * b))
                        of_x(2 * b + 1, Slot(n0, i, 4, 2 * b + 1))

            def out_phase(ln, n0, kt, parts):
                pe.matmul(ps[:, 6, :], zeros, x0, start=True, stop=False, skip_group_check=True)
                with pe.Fori(0, KD // 2) as i:
                    for b in range(2):
                        pe.wait_ge(y_done, KD * ln + 2 * i + b + 1)
                        for kh, (rh, rl) in enumerate(parts):
                            proj(4 + b, kt, Slot(n0, i, 4, 2 * b + kh), rh, rl, start=kh == 0, stop=kh == 1)
                    for b in range(2):
                        pe.wait_ge(y_done, KD * ln + 2 * i + b + 3)
                        pe.matmul(ps[:, 6, :], cn("mean_d"),
                                  x[:, bass.ds(2 * i + b, 1), :].rearrange("p a t -> p (a t)"),
                                  start=False, stop=False, skip_group_check=True)
                pe.matmul(ps[:, 6, :], zeros, x0, start=False, stop=True, skip_group_check=True).then_inc(mean_mm, 1)

            zeros = cn("zeros")
            x0 = x[:, 0, :]

            def norm_var(ln):
                for k in range(KD):
                    pe.wait_ge(sq_done, KD * ln + k + 1)
                    mm = pe.matmul(ps[:, 7, :], cn("mean_d"), sq[:, k, :], start=k == 0, stop=k == KD - 1)
                mm.then_inc(var_mm, 1)

            def head_mean(c, bank, src, banked):
                pe.wait_ge(hv_done, c + 1)
                banked()
                for z in range(HT):
                    mm = pe.matmul(ps[:, bank, :], cn("mean_256"), src[:, z, :], start=z == 0, stop=z == HT - 1)
                mm.then_inc(hmean_mm, 1)

            def head_var(c, bank, src):
                pe.wait_ge(hsq_done, c + 1)
                for z in range(HT):
                    mm = pe.matmul(ps[:, bank, :], cn("mean_256"), src(z), start=z == 0, stop=z == HT - 1)
                mm.then_inc(hvar_mm, 1)

            def even(n0):
                for t in range(KD + 2):
                    if t < KD:
                        if t >= 2:
                            pe.wait_ge(u_ev, t - 1)
                        of_x(t % 2, Slot(n0, 0, 2, t))
                    if t >= 2:
                        m = t - 2
                        pe.wait_ge(q_ev, m + 1)
                        pe.wait_ge(k_ev, m + 1)
                        pe.wait_ge(v_ev, m + 1)
                        for part, src in enumerate((q_all[:, m, :], k_all[:, m, :], vf[:, m % 2, :])):
                            for b in range(NB):
                                first, last = m == 0 and part == 0 and b == 0, m == KD - 1 and part == 2
                                mm = pe.matmul(ps[:, 6, b * 4 * NH:(b + 1) * 4 * NH], src[:, b * P:(b + 1) * P],
                                               wg[:, part * KD + m, :, :].rearrange("p y h -> p (y h)"),
                                               start=first, stop=last, skip_group_check=True)
                        if m == KD - 1:
                            mm.then_inc(gates_mm, 1)
                        if m >= 1:
                            pe.wait_ge(vt_ev, m)
                        for b in range(NB):
                            mm = pe.transpose(ps[:, 5, b * P:(b + 1) * P], vf[:, m % 2, b * P:(b + 1) * P], ident)
                        mm.then_inc(vt_mm, 1)
                    if 1 <= t <= KD:
                        m = t - 1
                        pe.wait_ge(bd_done, m + 1)
                        pe.wait_ge(c_done, m + 1)
                        if m >= 1:
                            pe.wait_ge(q_ev, m)
                        pe.matmul(ps[:, 2, :], bd[:, 0, :], cc[:, m % 2, :], start=True, stop=True).then_inc(q_mm, 1)
                        if m >= 1:
                            pe.wait_ge(k_ev, m)
                        pe.matmul(ps[:, 3, :], bd[:, 1, :], cc[:, m % 2, :], start=True, stop=True).then_inc(k_mm, 1)
                        if m >= 1:
                            pe.wait_ge(v_ev, m)
                        pe.matmul(ps[:, 4, :], bd[:, 2, :], um[:, m % 2, :, 2:2 + L], start=True,
                                  stop=True).then_inc(v_mm, 1)
                pe.wait_ge(gtok_ev, 1)
                for y in range(4):
                    for b in range(NB):
                        mm = pe.transpose(ps[0:NH, y, b * P:(b + 1) * P], gtok[:, b, y, :], ident)
                    mm.then_inc(rows_mm, 1)
                pe.wait_ge(g_done, 1)
                for d in range(2):
                    for b in range(NB):
                        o = (d * NB + b) * NH
                        mm = pe.transpose(ps[:, 4, o:o + NH], gi[:, d, b * P:(b + 1) * P], ident[0:NH, 0:NH])
                mm.then_inc(gT_mm, 1)
                pe.wait_ge(thr_done, 1)
                pe.wait_ge(gT_ev, 1)
                for h in range(NH):
                    if h >= 1:
                        pe.wait_ge(hv_done, h)
                    for d in range(2):
                        pe.matmul(ps[:, 2 + d, :], sel[:, h, :], negM[:, d, :], start=True, stop=True).then_inc(mb_mm, 1)
                    if h >= 1:
                        pe.wait_ge(abs_done, 2 * h)
                    if h >= 2:
                        pe.wait_ge(hvar_in, h - 1)
                    for d in range(2):
                        pe.matmul(ps[:, 4 + d, :], sel[:, h, :], thr[:, d, :], start=True, stop=True).then_inc(tb_mm, 1)
                    if h >= 1:
                        pe.wait_ge(s_done, 2 * h)
                    for q in range(SEQS):
                        for st in range(SB):
                            for z in range(HT):
                                o = q * L + st * P
                                mm = pe.matmul(ps[:, 6 + q, st * L:(st + 1) * L], k_all[:, HT * h + z, o:o + P],
                                               q_all[:, HT * h + z, q * L:(q + 1) * L],
                                               start=z == 0, stop=z == HT - 1)
                    mm.then_inc(qk_mm, 1)
                    if h >= 1:
                        pe.wait_ge(z_done, HT * h)
                    of_x(0, Slot(n0, 0, 2, KD + HT * h))
                    if h >= 1:
                        head_mean(h - 1, 5, hv, lambda: pe.wait_ge(tb_ev, 2 * h + 2))
                    for d, E in enumerate((Ef, Eb)):
                        pe.wait_ge(s_done, 2 * h + d + 1)
                        if d == 0:
                            pe.wait_ge(tb_ev, 2 * h + 1)
                        else:
                            pe.wait_ge(abs_done, 2 * h + 1)
                        for q in range(SEQS):
                            pe.matmul(ps[:, 4, q * L:(q + 1) * L], cn("ones"), E[:, q, 0:L], start=True, stop=False)
                            o = q * L + (P if d == 0 else 0)
                            mm = pe.matmul(ps[:, 4, o:o + P], cn("ones"), E[:, q, L:L + P], start=False, stop=True)
                        mm.then_inc(den_mm, 1)
                    of_x(1, Slot(n0, 0, 2, KD + HT * h + 1))
                    if h >= 1:
                        head_var(h - 1, 5, lambda z: q_all[:, HT * (h - 1) + z, :])
                    pe.wait_ge(att_done, h + 1)
                    for z in range(HT):
                        for q in range(SEQS):
                            for st in range(SB):
                                o = (HT * h + z) * P
                                mm = pe.matmul(ps[:, 2 + z, q * L:(q + 1) * L], vT[:, q * SB + st, o:o + P],
                                               att[:, q, st, :], start=st == 0, stop=st == SB - 1)
                    mm.then_inc(pv_mm, 1)
                pe.wait_ge(hvar_in, NH - 1)
                head_mean(NH - 1, 5, hv, lambda: None)
                head_var(NH - 1, 5, lambda z: q_all[:, HT * (NH - 1) + z, :])
                pe.wait_ge(z_done, HT * NH)

                n1 = n0 + 2 * KD

                def lru(i, j):
                    t = 2 * i + j
                    pe.wait_ge(lu_ev, t + 1)
                    of_x(0, Slot(n1, i, 4, 2 * j))
                    pe.wait_ge(gelu_done, t + 1)
                    of_x(1, Slot(n1, i, 4, 2 * j + 1))
                    pe.wait_ge(lx_done, t + 1)
                    pe.wait_ge(bd_in[j], 32 * (i + 1))
                    for g in range(4):
                        pe.wait_ge(lt_done, 4 * t + 1)
                        pe.matmul(ps[:, 2 + g, :], lbd[:, j, g, :], lx[:].rearrange("p s t -> p (s t)"),
                                  start=True, stop=True).then_inc(lg_mm, 1)

                with pe.Fori(0, KD // 2) as i:
                    lru(i, 0)
                    lru(i, 1)

            def odd(n0):
                hgrn_in = (0, 1, 2, 3, 4)
                for m in range(5):
                    of_x(m, Slot(n0, 0, 2, m))

                def mix(i, b):
                    h = 2 * i + b
                    read = [(a_q, h + 1), (a_sig, 4 * h + 2), (a_sig, 4 * h + 3), (a_i, h + 1), (a_g, h + 1)]

                    def nxt(k):
                        pe.wait_ge(*read[k])
                        of_x(hgrn_in[k], Slot(n0, i, 10, 5 * b + 5 + k))

                    pe.wait_ge(a_i, h + 1)
                    pe.wait_ge(mix_done, MIX_EVEN + h)
                    for b_ in range(NB):
                        mm = pe.transpose(ps[:, 7, b_ * P:(b_ + 1) * P], hi_[:, b_ * P:(b_ + 1) * P], ident)
                    mm.then_inc(a_vt_mm, 1)
                    pe.wait_ge(a_kq, h + 1)
                    pe.wait_ge(a_off, h + 1)
                    for b_ in range(NB):
                        c = slice(b_ * P, (b_ + 1) * P)
                        mm = pe.matmul(ps[:, 5, c], ks[:, c], hq[:, c], start=True, stop=True)
                    mm.then_inc(a_diag_mm, 1)
                    nxt(0)
                    for l in range(LEVELS):
                        pe.wait_ge(a_cp, LEVELS * h + l + 1)
                        if l == 0:
                            pe.wait_ge(a_vin, h + 1)
                        elif l == 1:
                            pe.wait_ge(a_diag, h + 1)
                        else:
                            pe.wait_ge(a_pred, LEVELS * h + l - 1)
                        for b_ in range(NB):
                            c = slice(b_ * P, (b_ + 1) * P)
                            mm = pe.matmul(ps[:, 6 - l % 2, c], KQ[:, 0, c], KQ[:, 1, c], start=True, stop=True)
                        mm.then_inc(a_lv_mm, 1)
                        if l in AHEAD:
                            nxt(AHEAD.index(l) + 1)
                    pe.wait_ge(a_up, LEVELS * h + LEVELS)
                    pe.wait_ge(a_pred, LEVELS * h + LEVELS - 1)
                    for q in range(SEQS):
                        c0, c1 = slice(q * L, q * L + P), slice(q * L + P, q * L + L)
                        pe.matmul(ps[:, 5, c0], Lo[:, 0, c0], Up[:, 1, c1], start=True, stop=True)
                        mm = pe.matmul(ps[:, 5, c1], Up[:, 0, c1], Lo[:, 1, c0], start=True, stop=True)
                    mm.then_inc(a_off_mm, 1)
                    pe.wait_ge(a_vt, h + 1)
                    pe.wait_ge(a_off, h + 2)
                    pe.wait_ge(a_pred, LEVELS * h + LEVELS)
                    for q in range(SEQS):
                        for tb in range(SB):
                            for st in range(SB):
                                o = q * L + tb * P
                                mm = pe.matmul(ps[:, 7, o:o + P], hvt[:, q * SB + st, :],
                                               hat[:, int(st != tb), q * SB + st, :], start=st == 0, stop=st == SB - 1)
                    mm.then_inc(a_pv, 1)
                    pe.wait_ge(a_sq, h + 1)
                    pe.matmul(ps[:, 6, :], cn("mean_128"), hsq[:], start=True, stop=True).then_inc(a_var, 1)

                with pe.Fori(0, HG // 2) as i:
                    mix(i, 0)
                    mix(i, 1)
                n1 = n0 + 5 * HG
                pe.wait_ge(mix_done, MIX_EVEN + HG)
                pe.wait_ge(a_vin, HG + 1)

                def ret(r, more):
                    c = NH + r

                    def slot(m, bank):
                        of_x(bank, Slot(n1, r, 8, m))

                    pe.wait_ge(r_q, r + 1)
                    slot(5, 0)
                    pe.wait_ge(r_k, r + 1)
                    pe.wait_ge(hvar_in, c)
                    for q in range(SEQS):
                        for st in range(SB):
                            for z in range(HT):
                                o = q * L + st * P
                                mm = pe.matmul(ps[:, 6 + q, st * L:(st + 1) * L], rk[:, z, o:o + P],
                                               rq[:, z, q * L:(q + 1) * L], start=z == 0, stop=z == HT - 1)
                    mm.then_inc(rqk_mm, 1)
                    slot(6, 1)
                    turn_v(r, 0)
                    slot(7, 2)
                    turn_v(r, 1)
                    pe.wait_ge(ratt_done, r + 1)
                    pe.wait_ge(rvt_ev, HT * r + HT + 1)
                    for z in range(HT):
                        for q in range(SEQS):
                            for st in range(SB):
                                mm = pe.matmul(ps[:, 3 + z, q * L:(q + 1) * L], rvt[:, q * SB + st, z, :],
                                               ratt[:, q, st, :], start=st == 0, stop=st == SB - 1)
                    mm.then_inc(pv_mm, 1)
                    if more:
                        slot(8, 0)
                    head_mean(c, 6, rhv, lambda: None)
                    if more:
                        pe.wait_ge(rz_done, HT * r + 1)
                        slot(9, 1)
                    head_var(c, 7, lambda z: rq[:, z, :])
                    if more:
                        pe.wait_ge(rz_done, HT * r + 2)
                        slot(10, 2)
                        slot(11, 3)
                        slot(12, 4)

                def turn_v(r, z):
                    pe.wait_ge(rv_ev, HT * r + z + 1)
                    pe.wait_ge(rvt_ev, HT * r + z + 1)
                    for b_ in range(NB):
                        mm = pe.transpose(ps[:, 5, b_ * P:(b_ + 1) * P], rv[:, b_ * P:(b_ + 1) * P], ident)
                    mm.then_inc(rvt_mm, 1)

                with pe.Fori(0, NH - 1) as r:
                    ret(r, True)
                ret(NH - 1, False)

            pe.wait_ge(const_in, 16 * 7)
            mixed = 0
            for st, (kind, n0, fi) in enumerate(stages):
                pe.wait_ge(xl_done, KD * (st + 1))
                if kind == "ffn":
                    ffn_in(fi, n0)
                    pe.wait_ge(h_done, FT * (fi + 1))
                    out_phase(st, n0 + IN_SLOTS, KH, [
                        (lambda k: hh[:, k, :], lambda k: hl[:, k, :]),
                        (lambda k: hh[:, KH + k, :], lambda k: hl[:, KH + k, :])])
                else:
                    (even if kind == "even" else odd)(n0)
                    mixed += MIX_EVEN if kind == "even" else MIX_ODD
                    pe.wait_ge(mix_done, mixed)
                    out_phase(st, n0 + own[kind], KD, [
                        (lambda k: yhA[:, k, :], lambda k: ylA[:, k, :]),
                        (lambda k: yhB[:, k, :], lambda k: ylB[:, k, :])])
                norm_var(st)

        @block.scalar
        def _(act):
            def split(kt, sl):
                act.wait_ge(raw_in[sl.par], 16 * (sl.half + 1))
                act.wait_ge(w_used, sl.n + 1)
                act.activation(wh[:, sl.par, 0:kt * P], raw[:, sl.par, 0:kt * P], ACT.Copy).then_inc(hi_done, 1)

            def used(sl):
                act.wait_ge(w_used, sl.n + 3)

            def ffn(fi, n0, nxt):
                def tile(i, b, after):
                    split(KD, Slot(n0, i, 4, 2 * b + 1))
                    split(after, Slot(n0, i, 4, 2 * b + 2))
                    used(Slot(n0, i, 4, 2 * b))
                    act.wait_ge(glu_done, FT * fi + 2 * i + b + 1)
                    act.activation(sg[:, b, :], ps[:, 2 * b, :], ACT.Silu).then_inc(silu_done, 1)

                with act.Fori(0, FT // 2 - 1) as i:
                    tile(i, 0, KD)
                    tile(i, 1, KD)
                tile(FT // 2 - 1, 0, KD)
                tile(FT // 2 - 1, 1, KH)
                out_splits(n0 + IN_SLOTS, KH, nxt)

            def out_splits(n0, kt, nxt):
                with act.Fori(0, OUT_SLOTS // 2 - 1) as i:
                    split(kt, Slot(n0, i, 2, 1))
                    split(kt, Slot(n0, i, 2, 2))
                split(kt, Slot(n0, OUT_SLOTS // 2 - 1, 2, 1))
                if nxt:
                    split(KD, Slot(n0, OUT_SLOTS // 2 - 1, 2, 2))

            def layer_norm(ln):
                for k in range(KD):
                    act.wait_ge(cen_done, KD * ln + k + 1)
                    act.activation(sq[:, k, :], x[:, k, :], ACT.Square).then_inc(sq_done, 1)
                act.wait_ge(var_in, ln + 1)
                act.activation(sq[:, 1, :], sq[:, 0, :], ACT.Sqrt).then_inc(rstd_done, 1)
                if ln < len(stages) - 1:
                    halves_of_x(ln)

            def halves_of_x(ln):
                for k in range(KD):
                    act.wait_ge(x_done, KD * ln + k + 1)
                    act.activation(xh[:, k, :], x[:, k, :], ACT.Copy).then_inc(xh_done, 1)

            def head_square(c, src, dst):
                act.wait_ge(hcen_done, c + 1)
                act.activation(dst, src[:], ACT.Square).then_inc(hsq_done, 1)

            def head_rstd(c, r):
                act.wait_ge(hvar_in, c + 1)
                act.activation(r, r, ACT.Sqrt).then_inc(hrstd_done, 1)

            def even(n0):
                for t in range(KD + 2):
                    if t < KD:
                        split(KD, Slot(n0, 0, 2, t + 1))
                        used(Slot(n0, 0, 2, t))
                        if t == 0:
                            act.wait_ge(um_zero, 1)
                        if t >= 2:
                            act.wait_ge(c_lin, t - 1)
                            act.wait_ge(v_mm, t - 1)
                        act.activation(um[:, t % 2, :, 2:2 + L], seqs(ps[:, t % 2, :]), ACT.Copy).then_inc(u_ev, 1)
                    if t >= 2:
                        m = t - 2
                        act.wait_ge(vt_mm, m + 1)
                        act.activation(vT[:, :, m * P:(m + 1) * P], blocks(ps[:, 5, :]), ACT.Copy).then_inc(vt_ev, 1)
                    if 1 <= t <= KD:
                        m = t - 1
                        act.wait_ge(q_mm, m + 1)
                        act.activation(q_all[:, m, :], ps[:, 2, :], ACT.Copy).then_inc(q_ev, 1)
                        act.wait_ge(k_mm, m + 1)
                        act.activation(k_all[:, m, :], ps[:, 3, :], ACT.Copy, scale=1.0 / 16.0).then_inc(k_ev, 1)
                        act.wait_ge(v_mm, m + 1)
                        act.activation(vf[:, m % 2, :], ps[:, 4, :], ACT.Copy).then_inc(v_ev, 1)
                    if t < KD:
                        act.wait_ge(c_lin, t + 1)
                        act.activation(seqs(cc[:, t % 2, :]), cv[:], ACT.Silu, bias=vc("ml_cb", t)).then_inc(c_done, 1)
                act.wait_ge(gates_mm, 1)
                act.activation(gtok[:].rearrange("p b y h -> p (b y h)"), ps[:, 6, 0:NB * 4 * NH],
                               ACT.Copy).then_inc(gtok_ev, 1)
                for d in range(2):
                    act.wait_ge(rows_mm, 2 * d + 2)
                    act.activation(gi[:, d, :], ps[0:NH, 2 * d, :], ACT.Identity,
                                   bias=gb[:, 2 * d:2 * d + 1]).then_inc(rows_a, 1)
                    act.activation(gf[:, d, :], ps[0:NH, 2 * d + 1, :], ACT.Identity,
                                   bias=gb[:, 2 * d + 1:2 * d + 2]).then_inc(rows_a, 1)
                act.wait_ge(rows_a, 4)
                act.activation(g1[:], gf[:], ACT.Abs).then_inc(rows_a, 1)
                act.wait_ge(rows_a, 5)
                act.activation(g1[:], g1[:], ACT.Exp, scale=-1.0).then_inc(rows_a, 1)
                act.wait_ge(rows_a, 6)
                act.activation(g2[:], g1[:], ACT.Ln, bias=1.0).then_inc(rows_a, 1)
                act.wait_ge(gT_mm, 1)
                act.activation(gT[:].rearrange("p d b h -> p (d b h)"), ps[:, 4, 0:2 * NB * NH],
                               ACT.Copy).then_inc(gT_ev, 1)
                act.wait_ge(marg_done, 1)
                act.activation(thr[:], g1[:], ACT.Exp).then_inc(thr_done, 1)
                for h in range(NH):
                    for d in range(2):
                        act.wait_ge(tb_mm, 2 * h + d + 1)
                        if h >= 1:
                            act.wait_ge(att_done, h)
                        act.activation(rec[:, d, :], ps[:, 4 + d, :], ACT.Copy).then_inc(tb_ev, 1)
                    for d, E in enumerate((Ef, Eb)):
                        act.wait_ge(t_done, 2 * h + d + 1)
                        act.activation(E[:], E[:], ACT.Exp).then_inc(e_done, 1)
                    split(KD, Slot(n0, 0, 2, KD + HT * h + 1))
                    if h >= 1:
                        head_square(h - 1, hv, q_all[:, HT * (h - 1):HT * h, :])
                    for d in range(2):
                        act.wait_ge(den_mm, 2 * h + d + 1)
                        if h + d:
                            act.wait_ge(dmax_done, 2 * h + d)
                        act.activation(dab[:], ps[:, 4, :], ACT.Abs).then_inc(abs_done, 1)
                    split(KD, Slot(n0, 0, 2, KD + HT * h + 2))
                    if h >= 1:
                        head_rstd(h - 1, rs[:])
                    if h >= 1:
                        act.wait_ge(mix_done, h)
                    for z in range(HT):
                        used(Slot(n0, 0, 2, KD + HT * h + z))
                        act.activation(zs[:, z, :], ps[:, z, :], ACT.Sigmoid).then_inc(z_done, 1)
                    act.wait_ge(pv_mm, h + 1)
                    act.activation(hv[:], ps[:, 2:4, :], ACT.Copy).then_inc(hv_done, 1)
                head_square(NH - 1, hv, q_all[:, HT * (NH - 1):HT * NH, :])
                head_rstd(NH - 1, rs[:])

                n1 = n0 + 2 * KD
                act.wait_ge(lzero, 1)

                def lru(i, j):
                    t = 2 * i + j
                    split(KD, Slot(n1, i, 4, 2 * j + 1))
                    used(Slot(n1, i, 4, 2 * j))
                    act.activation(lum[:, :, 2:2 + L], seqs(ps[:, 0, :]), ACT.Copy).then_inc(lu_ev, 1)
                    split(KD, Slot(n1, i, 4, 2 * j + 2))
                    used(Slot(n1, i, 4, 2 * j + 1))
                    act.wait_ge(mix_done, NH + t)
                    act.activation(lgl[:], ps[:, 1, :], ACT.Gelu_apprx_tanh).then_inc(gelu_done, 1)
                    act.wait_ge(lix_done, 2 * t + 1)
                    for g in range(2):
                        for d in range(2):
                            act.wait_ge(lg_mm, 4 * t + 2 * g + d + 2)
                            act.activation(th[:, g, d, :], ps[:, 2 + 2 * g + d, :], ACT.Tanh, scale=0.5,
                                           bias=hbias[:, bass.ds((2 * g + d) * KD + t, 1)]).then_inc(lt_done, 1)
                    act.wait_ge(lt_done, 4 * t + 3)
                    for d in range(2):
                        act.activation(la[:, d, :], th[:, 0, d, :], ACT.Exp,
                                       scale=sp[:, 1, bass.ds(d * KD + t, 1)],
                                       bias=sp[:, 1, bass.ds(d * KD + t, 1)]).then_inc(la_done, 1)
                    for d in range(2):
                        act.activation(lw[:, d, :], th[:, 0, d, :], ACT.Tanh,
                                       scale=sp[:, 2, bass.ds(d * KD + t, 1)],
                                       bias=sp[:, 2, bass.ds(d * KD + t, 1)]).then_inc(lw_done, 1)
                    act.wait_ge(lq_done, t + 1)
                    act.activation(lr[:], lq[:], ACT.Sqrt, scale=0.5).then_inc(lsq_done, 1)

                with act.Fori(0, KD // 2) as i:
                    lru(i, 0)
                    lru(i, 1)

            def odd(n0):
                for m in range(1, 6):
                    split(KD, Slot(n0, 0, 2, m))

                def mix(i, b):
                    h = 2 * i + b

                    def ahead(k):
                        split(KD, Slot(n0, i, 10, 5 * b + 5 + k + 1))

                    act.wait_ge(mix_done, MIX_EVEN + h)
                    used(Slot(n0, i, 10, 5 * b))
                    act.activation(ho[:], ps[:, 0, :], ACT.Sigmoid).then_inc(a_sig, 1)
                    for d in range(2):
                        used(Slot(n0, i, 10, 5 * b + 1 + d))
                        act.activation(TA[:, d, :], ps[:, 1 + d, :], ACT.Sigmoid).then_inc(a_sig, 1)
                    used(Slot(n0, i, 10, 5 * b + 4))
                    act.activation(hgs[:], ps[:, 4, :], ACT.Sigmoid).then_inc(a_sig, 1)
                    act.activation(hi_[:], ps[:, 3, :], ACT.Copy).then_inc(a_i, 1)
                    act.wait_ge(a_vt_mm, h + 1)
                    act.activation(hvt[:], blocks(ps[:, 7, :]), ACT.Copy).then_inc(a_vt, 1)
                    ahead(0)
                    for l in range(LEVELS):
                        if l == 0:
                            act.wait_ge(a_kq, h + 1)
                        else:
                            act.wait_ge(a_up, LEVELS * h + l)
                            act.wait_ge(a_lv_mm, LEVELS * h + l)
                        act.activation(halves(KQ[:], 1 << l)[0], halves(Lo[:], 1 << l)[0], ACT.Copy)
                        act.activation(halves(KQ[:], 1 << l)[1], halves(Up[:], 1 << l)[1], ACT.Copy).then_inc(a_cp, 1)
                        if l in AHEAD:
                            ahead(AHEAD.index(l) + 1)
                    act.wait_ge(a_off_mm, h + 1)
                    act.activation(hat[:, 1, :, :], blocks(ps[:, 5, :]), ACT.Copy).then_inc(a_off, 1)
                    act.wait_ge(a_pv, h + 2)
                    act.activation(hsq[:], ps[:, 7, :], ACT.Square).then_inc(a_sq, 1)
                    act.wait_ge(a_vin, h + 2)
                    act.activation(hrs[:], hrs[:], ACT.Sqrt).then_inc(a_rstd, 1)

                with act.Fori(0, HG // 2) as i:
                    mix(i, 0)
                    mix(i, 1)
                n1 = n0 + 5 * HG

                def ret(r, more):
                    c = NH + r

                    def sl(m):
                        return Slot(n1, r, 8, m)

                    act.wait_ge(rvt_mm, HT * r + 1)
                    used(sl(4))
                    act.activation(rv[:], ps[:, 4, :], ACT.Copy).then_inc(rv_ev, 1)
                    split(KD, sl(6))
                    split(KD, sl(7))
                    act.wait_ge(rvt_mm, HT * r + 2)
                    act.activation(rvt[:, :, 0, :], blocks(ps[:, 5, :]), ACT.Copy).then_inc(rvt_ev, 1)
                    act.activation(rv[:], ps[:, 0, :], ACT.Copy).then_inc(rv_ev, 1)
                    split(KD, sl(8))
                    act.wait_ge(mix_done, MIX_EVEN + HG + r)
                    for z in range(HT):
                        used(sl(6 + z))
                        act.activation(rzs[:, z, :], ps[:, 1 + z, :], ACT.Sigmoid).then_inc(rz_ev, 1)
                    act.wait_ge(rvt_mm, HT * r + 3)
                    act.activation(rvt[:, :, 1, :], blocks(ps[:, 5, :]), ACT.Copy).then_inc(rvt_ev, 1)
                    act.wait_ge(pv_mm, c + 1)
                    act.activation(rhv[:], ps[:, 3:5, :], ACT.Copy).then_inc(hv_done, 1)
                    if more:
                        split(KD, sl(9))
                    head_square(c, rhv, rq[:])
                    if more:
                        split(KD, sl(10))
                    head_rstd(c, rrec[:])
                    if more:
                        split(KD, sl(11))
                        split(KD, sl(12))
                        split(KD, sl(13))

                with act.Fori(0, NH - 1) as r:
                    ret(r, True)
                ret(NH - 1, False)

            act.sem_inc(hi_done, 2)
            for s in (lu_ev, gelu_done, lt_done, a_off, rvt_ev):
                act.sem_inc(s, 1)
            act.wait_ge(const_in, 16 * 7)
            lam = vc("lam", 0, 2 * KD)
            act.activation(sp[:, 1, :], lam, ACT.Abs).then_inc(prep_a, 1)
            act.wait_ge(prep_a, 1)
            act.activation(sp[:, 1, :], sp[:, 1, :], ACT.Exp, scale=-1.0).then_inc(prep_a, 1)
            act.wait_ge(prep_a, 2)
            act.activation(sp[:, 1, :], sp[:, 1, :], ACT.Ln, bias=1.0).then_inc(prep_a, 1)
            act.wait_ge(prep_d, 1)
            act.activation(lb[:, 0:2, :], lb[:, 0:2, :], ACT.Exp).then_inc(prep_a, 1)
            act.wait_ge(x_in, 16)
            for k in range(KD):
                act.activation(xh[:, k, :], x[:, k, :], ACT.Copy).then_inc(xh_done, 1)
            split(KD, Slot(0, 0, 2, 0))
            for st, (kind, n0, fi) in enumerate(stages):
                more = st < len(stages) - 1
                if kind == "ffn":
                    ffn(fi, n0, more)
                elif kind == "even":
                    even(n0)
                    out_splits(n0 + EV_SLOTS, KD, more)
                else:
                    odd(n0)
                    out_splits(n0 + OD_SLOTS, KD, more)
                layer_norm(st)

        @block.vector
        def _(dve):
            steps = [0]

            def step(ins, n=None):
                steps[0] += 1
                ins.then_inc(step_done, 1)
                dve.wait_ge(step_done, steps[0] + loop[0])

            loop = [0]

            class passes:

                def __init__(self, var, n, per):
                    self.var, self.n, self.per = var, n, per

                def __enter__(self):
                    loop[0], self.at = self.per * self.var, steps[0]

                def __exit__(self, *_):
                    assert steps[0] - self.at == self.per, (steps[0] - self.at, self.per)
                    steps[0] += self.per * (self.n - 1)
                    loop[0] = 0

            def ffn(fi, n0):
                n_ = FT // 2
                with dve.Fori(0, n_) as i, passes(i, n_, 2):
                    for b in range(2):
                        j = 2 * i + b
                        dve.wait_ge(silu_done, FT * fi + j + 1)
                        dve.wait_ge(w_used, Slot(n0, i, 4, 2 * b + 1).n + 3)
                        dve.scalar_tensor_tensor(hf[:, b, :], sg[:, b, :], 0.5, ps[:, 2 * b + 1, :], ALU.mult,
                                                 ALU.mult).then_inc(glu_done, 1)
                        dve.wait_ge(glu_done, FT * fi + j + 3)
                        hh_j = hh[:, bass.ds(j, 1), :].rearrange("p a t -> p (a t)")
                        step(dve.tensor_copy(hh_j, hf[:, b, :]))
                        dve.tensor_tensor(hl[:, bass.ds(j, 1), :].rearrange("p a t -> p (a t)"), hf[:, b, :],
                                          hh_j.bitcast(F32), ALU.subtract).then_inc(h_done, 1)

            def residual(ln, n0):
                with dve.Fori(0, KD // 2) as i:
                    for b in range(2):
                        dve.wait_ge(w_used, Slot(n0, i, 4, 2 * b + 1).n + 3)
                        x_k = x[:, bass.ds(2 * i + b, 1), :].rearrange("p a t -> p (a t)")
                        dve.scalar_tensor_tensor(x_k, x_k, ALPHA, ps[:, 4 + b, :], ALU.mult,
                                                 ALU.add).then_inc(y_done, 1)

            def layer_norm(ln):
                dve.wait_ge(mean_mm, ln + 1)
                for k in range(KD):
                    dve.tensor_tensor(x[:, k, :], x[:, k, :], ps[:, 6, :], ALU.subtract).then_inc(cen_done, 1)
                dve.wait_ge(var_mm, ln + 1)
                step(dve.tensor_scalar(sq[:, 0, :], ps[:, 7, :], EPS, None, ALU.add))
                dve.reciprocal(sq[:, 0, :], sq[:, 0, :]).then_inc(var_in, 1)
                dve.wait_ge(rstd_done, ln + 1)
                for k in range(KD):
                    step(dve.tensor_tensor(x[:, k, :], x[:, k, :], sq[:, 1, :], ALU.mult))
                    dve.tensor_scalar(x[:, k, :], x[:, k, :], vc("ln_g", ln * KD + k), vc("ln_b", ln * KD + k),
                                      ALU.mult, ALU.add).then_inc(x_done, 1)
                    if k >= 1 and ln < len(stages) - 1:
                        low_of_x(ln + 1, k - 1)
                if ln < len(stages) - 1:
                    low_of_x(ln + 1, KD - 1)

            def low_of_x(n, k):
                dve.wait_ge(xh_done, KD * n + k + 1)
                dve.tensor_tensor(xl[:, k, :], x[:, k, :], xh[:, k, :].bitcast(F32), ALU.subtract).then_inc(xl_done, 1)

            def head_cen(c, bank, v):
                dve.wait_ge(hmean_mm, c + 1)
                dve.tensor_tensor(v[:], v[:], ps[:, bank, None, :].to_broadcast([P, HT, T]),
                                  ALU.subtract).then_inc(hcen_done, 1)

            def head_norm(c, bank, v, r, g, tile, z_, yh, yl):
                dve.wait_ge(hvar_mm, c + 1)
                step(dve.tensor_scalar(r, ps[:, bank, :], EPS, None, ALU.add))
                dve.reciprocal(r, r).then_inc(hvar_in, 1)
                dve.wait_ge(hrstd_done, c + 1)
                step(dve.tensor_tensor(v[:], v[:], r[:, None, :].to_broadcast([P, HT, T]), ALU.mult))
                for z in range(HT):
                    ins = dve.scalar_tensor_tensor(v[:, z, :], v[:, z, :], vc(g, tile + z), z_[:, z, :], ALU.mult,
                                                   ALU.mult)
                step(ins)
                y_h = yh[:, bass.ds(tile, HT), :]
                step(dve.tensor_copy(y_h, v[:]))
                dve.tensor_tensor(yl[:, bass.ds(tile, HT), :], v[:], y_h.bitcast(F32),
                                  ALU.subtract).then_inc(mix_done, 1)

            def conv(src, dst, w, b, t):
                for j in range(4):
                    wj = vc(w, KD * j + t)
                    if j:
                        ins = dve.scalar_tensor_tensor(dst[:], src[:, :, j:j + L], wj, dst[:], ALU.mult, ALU.add)
                    elif b:
                        ins = dve.tensor_scalar(dst[:], src[:, :, 0:L], wj, vc(b, t), ALU.mult, ALU.add)
                    else:
                        ins = dve.tensor_scalar(dst[:], src[:, :, 0:L], wj, None, ALU.mult)
                    if j < 3:
                        step(ins)
                return ins

            def even(n0):
                dve.memset(um[:], 0.0).then_inc(um_zero, 1)
                for t in range(KD):
                    if t >= 1:
                        dve.wait_ge(v_mm, t)
                    for j in range(3):
                        ins = dve.tensor_tensor(bd[:, j, :].rearrange("p (b d) -> p b d", d=4),
                                                w4[:, j, t, None, :].to_broadcast([P, 32, 4]),
                                                cn("bd")[:, :, None].to_broadcast([P, 32, 4]), ALU.mult)
                    ins.then_inc(bd_done, 1)
                    dve.wait_ge(u_ev, t + 1)
                    if t >= 1:
                        dve.wait_ge(c_done, t)
                    conv(um[:, t % 2], cv, "ml_cw", None, t).then_inc(c_lin, 1)
                dve.wait_ge(rows_a, 7)
                dve.memset(one[:], 1.0)
                step(dve.scalar_tensor_tensor(gf[:], gf[:], 0.0, g2[:], ALU.min, ALU.subtract))

                def scan(dst, d0, d1, op0, op1):
                    for q in range(SEQS):
                        for d in range(2):
                            def way(t_):
                                return t_ if d == 0 else t_[:, ::-1]
                            c = slice(q * L, (q + 1) * L)
                            ins = dve.tensor_tensor_scan(way(dst[:, d, c]), way(d0(d, c)), way(d1(d, c)), 0.0, op0, op1)
                    return ins

                step(scan(g2, lambda d, c: one[:], lambda d, c: gf[:, d, c], ALU.mult, ALU.add))
                dve.tensor_tensor(gi[:], gi[:], g2[:], ALU.subtract).then_inc(g_done, 1)
                dve.wait_ge(g_done, 1)
                step(scan(g1, lambda d, c: gi[:, d, c], lambda d, c: gi[:, d, c], ALU.max, ALU.max))
                step(dve.tensor_scalar(negM[:], g1[:], -1.0, None, ALU.mult))
                step(dve.tensor_tensor(g1[:], negM[:], g2[:], ALU.subtract))
                dve.tensor_scalar(g1[:], g1[:], 88.0, None, ALU.min).then_inc(marg_done, 1)
                dve.wait_ge(gT_ev, 1)
                for h in range(NH):
                    for d, E in enumerate((Ef, Eb)):
                        dve.wait_ge(mb_mm, 2 * h + d + 1)
                        for q in range(SEQS):
                            own_, other = (0, 1) if d == 0 else (1, 0)
                            full, part = gT[:, d, q * SB + own_, h:h + 1], gT[:, d, q * SB + other, h:h + 1]
                            dve.scalar_tensor_tensor(E[:, q, 0:L], ps[:, 2 + d, q * L:(q + 1) * L], full,
                                                     tri[:, d * L:(d + 1) * L], ALU.add, ALU.min)
                            o = q * L + (P if d == 0 else 0)
                            m = 0 if d == 0 else L + P
                            ins = dve.scalar_tensor_tensor(E[:, q, L:L + P], ps[:, 2 + d, o:o + P], part,
                                                           tri[:, m:m + P], ALU.add, ALU.min)
                        ins.then_inc(t_done, 1)
                    dve.wait_ge(qk_mm, h + 1)
                    for d, E in enumerate((Ef, Eb)):
                        dve.wait_ge(e_done, 2 * h + d + 1)
                        o1, o2 = (0, L + P) if d == 0 else (L, 0)
                        dve.tensor_tensor(E[:, :, 0:L], E[:, :, 0:L], ps[:, 6:8, o1:o1 + L], ALU.mult)
                        dve.tensor_tensor(E[:, :, L:L + P], E[:, :, L:L + P], ps[:, 6:8, o2:o2 + P],
                                          ALU.mult).then_inc(s_done, 1)
                    if h >= 1:
                        head_cen(h - 1, 5, hv)
                    for d, E in enumerate((Ef, Eb)):
                        dve.wait_ge(abs_done, 2 * h + d + 1)
                        dve.tensor_tensor(rec[:, d, :], rec[:, d, :], dab[:], ALU.max).then_inc(dmax_done, 1)
                        dve.wait_ge(dmax_done, 2 * h + d + 1)
                        step(dve.reciprocal(rec[:, d, :], rec[:, d, :]))
                        r = seqs(rec[:, d, :])
                        if d == 0:
                            dve.tensor_tensor(att[:, :, 0, :], E[:, :, 0:L], r, ALU.mult)
                            step(dve.tensor_tensor(att[:, :, 1, P:L], E[:, :, L:L + P], r[:, :, P:L], ALU.mult))
                        else:
                            dve.tensor_tensor(att[:, :, 1, 0:P], E[:, :, 0:P], r[:, :, 0:P], ALU.mult)
                            dve.tensor_tensor(E[:, :, P:L], E[:, :, P:L], r[:, :, P:L], ALU.mult)
                            step(dve.tensor_tensor(E[:, :, L:L + P], E[:, :, L:L + P], r[:, :, 0:P], ALU.mult))
                            dve.tensor_tensor(att[:, :, 1, P:L], att[:, :, 1, P:L], E[:, :, P:L], ALU.add)
                            dve.tensor_tensor(att[:, :, 0, 0:P], att[:, :, 0, 0:P], E[:, :, L:L + P],
                                              ALU.add).then_inc(att_done, 1)
                    if h >= 1:
                        head_norm(h - 1, 5, hv, rs[:], "ml_g", HT * (h - 1), zs, yhA, ylA)
                head_cen(NH - 1, 5, hv)
                head_norm(NH - 1, 5, hv, rs[:], "ml_g", HT * (NH - 1), zs, yhA, ylA)

                dve.memset(lbd[:], 0.0)
                dve.memset(lum[:], 0.0).then_inc(lzero, 1)
                with dve.Fori(0, KD) as t, passes(t, KD, 10):
                    dve.wait_ge(lu_ev, t + 2)
                    dve.wait_ge(lg_mm, 4 * t + 1)
                    dve.wait_ge(lix_done, 2 * t + 1)
                    conv(lum, lx, "lru_cw", "lru_cb", t).then_inc(lx_done, 1)
                    dve.wait_ge(lw_done, 2 * t + 2)
                    step(dve.tensor_scalar(lr[:], lw[:], 1.0, None, ALU.add))
                    step(dve.reciprocal(lr[:], lr[:]))
                    dve.tensor_tensor(lq[:], lw[:], lr[:], ALU.mult).then_inc(lq_done, 1)
                    dve.wait_ge(lsq_done, t + 1)
                    dve.wait_ge(lix_done, 2 * t + 3)
                    step(dve.tensor_tensor(lq[:], lr[:], lix[:], ALU.mult))
                    for q in range(SEQS):
                        c = slice(q * L, (q + 1) * L)
                        dve.tensor_tensor_scan(lw[:, 0, c], la[:, 0, c], lq[:, 0, c], 0.0, ALU.mult, ALU.add)
                        ins = dve.tensor_tensor_scan(lw[:, 1, c][:, ::-1], la[:, 1, c][:, ::-1],
                                                     lq[:, 1, c][:, ::-1], 0.0, ALU.mult, ALU.add)
                    step(ins)
                    step(dve.tensor_tensor(lw[:, 0, :], lw[:, 0, :], lw[:, 1, :], ALU.add))
                    step(dve.tensor_tensor(lw[:, 0, :], lw[:, 0, :], lgl[:], ALU.mult))
                    y_h = yhB[:, bass.ds(t, 1), :].rearrange("p a t -> p (a t)")
                    step(dve.tensor_copy(y_h, lw[:, 0, :]))
                    dve.tensor_tensor(ylB[:, bass.ds(t, 1), :].rearrange("p a t -> p (a t)"), lw[:, 0, :],
                                      y_h.bitcast(F32), ALU.subtract).then_inc(mix_done, 1)

            def odd(n0):
                def mix(i, b):
                    h = 2 * i + b
                    dve.wait_ge(a_sig, 4 * h + 1)
                    dve.tensor_tensor(hq[:], ho[:], ps[:, 0, :], ALU.mult).then_inc(a_q, 1)
                    dve.wait_ge(a_sig, 4 * h + 3)
                    dve.wait_ge(a_off, h + 1)
                    step(dve.tensor_scalar(TA[:, 0:2, :], TA[:, 0:2, :], lb[:, 1, bass.ds(h, 1)],
                                           lb[:, 0, bass.ds(h, 1)], ALU.mult, ALU.add))
                    dve.tensor_copy(TA[:, 2, :], TA[:, 0, :])
                    dve.tensor_scalar(Lo[:, 0, :], TA[:, 0, :], -1.0, 1.0, ALU.mult, ALU.add)
                    dve.tensor_scalar(Up[:, 0, :], TA[:, 1, :], -1.0, 1.0, ALU.mult, ALU.add)
                    dve.wait_ge(a_q, h + 1)
                    dve.tensor_tensor(Lo[:, 1, :], hq[:], TA[:, 1, :], ALU.mult)
                    step(dve.tensor_tensor(Up[:, 1, :], hq[:], TA[:, 0, :], ALU.mult))
                    dve.tensor_tensor(ks[:], Lo[:, 0, :], Up[:, 0, :], ALU.add).then_inc(a_kq, 1)
                    dve.wait_ge(a_sig, 4 * h + 4)
                    dve.tensor_tensor(hgs[:], hgs[:], ps[:, 4, :], ALU.mult).then_inc(a_g, 1)
                    dve.wait_ge(a_diag_mm, h + 1)
                    dve.wait_ge(a_pv, h + 1)
                    dve.tensor_tensor(hat[:, 0, :, :], blocks(ps[:, 5, :]), ident[:, None, :].to_broadcast([P, NB, P]),
                                      ALU.mult).then_inc(a_diag, 1)
                    dve.wait_ge(a_diag, h + 1)
                    for l in range(LEVELS):
                        B, cur, nxt_ = 1 << l, (TA, TB)[l % 2], (TB, TA)[l % 2]
                        n = T // B
                        dve.wait_ge(a_cp, LEVELS * h + l + 1)
                        pairs = cur[:, :, 0:n].rearrange("p r (n two) -> p r n two", two=2)
                        low, high = pairs[:, :, :, 0], pairs[:, :, :, 1]
                        lo_, up_ = halves(Lo[:], B)[0], halves(Up[:], B)[1]
                        dve.tensor_tensor(lo_, lo_, spread(high[:, 0:2, :], B), ALU.mult)
                        if l == LEVELS - 1:
                            dve.wait_ge(a_lv_mm, LEVELS * h + l + 1)
                        dve.tensor_tensor(up_, up_, spread(low[:, 1:3, :], B), ALU.mult).then_inc(a_up, 1)
                        if l < LEVELS - 1:
                            dve.wait_ge(a_lv_mm, LEVELS * h + l + 1)
                            dve.tensor_tensor(nxt_[:, :, 0:n // 2], low, high, ALU.mult)
                        dve.copy_predicated(hat[:, 0, :, :], pmask[:, l, None, :].to_broadcast([P, NB, P]),
                                            blocks(ps[:, 6 - l % 2, :])).then_inc(a_pred, 1)
                        dve.wait_ge(a_pred, LEVELS * h + l + 1)
                    dve.wait_ge(a_var, h + 1)
                    step(dve.tensor_scalar(hrs[:], ps[:, 6, :], EPS, None, ALU.add))
                    dve.reciprocal(hrs[:], hrs[:]).then_inc(a_vin, 1)
                    dve.wait_ge(a_rstd, h + 1)
                    step(dve.scalar_tensor_tensor(ho[:], ps[:, 7, :], vc("hg_g", h), hrs[:], ALU.mult, ALU.mult))
                    step(dve.tensor_tensor(ho[:], ho[:], hgs[:], ALU.mult))
                    y_h = yhA[:, bass.ds(h, 1), :].rearrange("p a t -> p (a t)")
                    step(dve.tensor_copy(y_h, ho[:]))
                    dve.tensor_tensor(ylA[:, bass.ds(h, 1), :].rearrange("p a t -> p (a t)"), ho[:],
                                      y_h.bitcast(F32), ALU.subtract).then_inc(mix_done, 1)

                n_ = HG // 2
                with dve.Fori(0, n_) as i, passes(i, n_, 12):
                    mix(i, 0)
                    mix(i, 1)
                n1 = n0 + 5 * HG

                def rope(r, bank, dst, done, m):
                    dve.wait_ge(w_used, m.n + 3)
                    t1, t2 = seqs(ps[:, bank, :]), seqs(ps[:, bank + 1, :])
                    co, si = (v[:, None, :].to_broadcast([P, SEQS, L]) for v in (cos, sin))
                    for k, (t_, v) in enumerate(((t1, co), (t2, si), (t1, si), (t2, co))):
                        ins = dve.tensor_tensor(seqs(rt[:, k, :]), t_, v, ALU.mult)
                    step(ins)
                    dve.tensor_tensor(dst[:, 0, :], rt[:, 0, :], rt[:, 1, :], ALU.subtract)
                    dve.tensor_tensor(dst[:, 1, :], rt[:, 2, :], rt[:, 3, :], ALU.add).then_inc(done, 1)
                    dve.wait_ge(done, r + 1)

                dve.wait_ge(odd_in, 16)

                def ret(r):
                    c = NH + r
                    dve.wait_ge(hvar_mm, c)
                    rope(r, 0, rq, r_q, Slot(n1, r, 8, 1))
                    rope(r, 2, rk, r_k, Slot(n1, r, 8, 3))
                    dve.wait_ge(rqk_mm, r + 1)
                    dve.wait_ge(pv_mm, c)
                    for st in range(SB):
                        decay = odc[:, bass.ds(2 * L + 3 * P * r + P * (1 - st), L)]
                        ins = dve.tensor_tensor(ratt[:, :, st, :], ps[:, 6:8, st * L:(st + 1) * L],
                                                decay[:, None, :].to_broadcast([P, SEQS, L]), ALU.mult)
                    ins.then_inc(ratt_done, 1)
                    for z in range(HT):
                        dve.wait_ge(rz_ev, HT * r + z + 1)
                        dve.tensor_tensor(rzs[:, z, :], rzs[:, z, :], ps[:, 1 + z, :], ALU.mult).then_inc(rz_done, 1)
                    head_cen(c, 6, rhv)
                    head_norm(c, 7, rhv, rrec[:], "ret_g", HT * r, rzs, yhB, ylB)

                with dve.Fori(0, NH) as r, passes(r, NH, 6):
                    ret(r)

            dve.sem_inc(glu_done, 2)
            dve.sem_inc(a_vin, 1)
            dve.sem_inc(y_done, 2)
            dve.wait_ge(const_in, 16 * 7)
            l0, l1 = vc("lb", 0, KD), vc("lb", KD, KD)
            step(dve.tensor_tensor(lb[:, 2, :], l0, l1, ALU.max))
            dve.tensor_copy(pmask[:], mask_f[:])
            dve.tensor_tensor(lb[:, 0, :], l0, lb[:, 2, :], ALU.subtract)
            dve.tensor_tensor(lb[:, 1, :], l1, lb[:, 2, :], ALU.subtract).then_inc(prep_d, 1)
            dve.tensor_scalar(hbias[:], vec[:, bass.ds(VEC["b_a"][0], 4 * KD)], 0.5, None, ALU.mult)
            dve.wait_ge(prep_a, 3)
            step(dve.tensor_scalar(sp[:, 2, :], vc("lam", 0, 2 * KD), -1.0, 0.0, ALU.mult, ALU.max))
            step(dve.tensor_tensor(sp[:, 0, :], sp[:, 2, :], sp[:, 1, :], ALU.add))
            dve.tensor_scalar(sp[:, 1, :], sp[:, 0, :], -4.0, None, ALU.mult)
            dve.tensor_scalar(sp[:, 2, :], sp[:, 0, :], 4.0, None, ALU.mult)
            dve.wait_ge(prep_a, 4)
            step(dve.tensor_tensor(lb[:, 2, :], lb[:, 0, :], lb[:, 1, :], ALU.add))
            step(dve.reciprocal(lb[:, 2, :], lb[:, 2, :]))
            step(dve.tensor_tensor(lb[:, 0, :], lb[:, 1, :], lb[:, 2, :], ALU.mult))
            step(dve.tensor_scalar(lb[:, 1, :], lb[:, 0, :], -1.0, 1.0, ALU.mult, ALU.add))
            for k in range(KD):
                low_of_x(0, k)
            for st, (kind, n0, fi) in enumerate(stages):
                if kind == "ffn":
                    ffn(fi, n0)
                elif kind == "even":
                    even(n0)
                else:
                    odd(n0)
                residual(st, n0 + own[kind])
                layer_norm(st)


def _host_constants():
    s, t = np.arange(P)[:, None], np.arange(P)[None, :]
    con = np.zeros((P, NC), np.float32)

    def put(name, v):
        o, n = CON[name]
        con[:, o:o + n] = v

    put("ident", s == t)
    put("mean_d", 1.0 / D)
    put("mean_256", 1.0 / (HT * P))
    put("mean_128", 1.0 / P)
    put("ones", 1.0)
    tri = np.zeros((P, 2 * L), np.float32)
    tri[:, 0:P][s > t] = -1e30
    tri[:, L + P:][s < t] = -1e30
    put("tri", tri)
    put("bd", np.arange(P)[:, None] // 4 == np.arange(32)[None, :])
    pmask = np.zeros((P, LEVELS, P), np.float32)
    for l in range(LEVELS):
        pmask[:, l, :] = (s >> (l + 1) == t >> (l + 1)) & (s >> l != t >> l)
    sel = np.zeros((NH, NH, P), np.float32)
    for h in range(NH):
        sel[h, h, :] = 1.0
    half = HT * P // 2
    ang = np.arange(L, dtype=np.float64)[None, :] * 10000.0 ** (-np.arange(half, dtype=np.float64)[:, None] / half)
    lg = np.log(1.0 - 2.0 ** (-5.0 - np.arange(NH, dtype=np.float64)))
    decay = np.zeros((NH, P, 3 * P))
    for h in range(NH):
        def both(diff):
            fwd = np.where(diff >= 0, np.exp(np.minimum(diff * lg[h], 0.0)), 0.0)
            bwd = np.where(diff <= 0, np.exp(np.minimum(-diff * lg[NH - 1 - h], 0.0)), 0.0)
            return (fwd + bwd) / np.sqrt(HT * P)
        decay[h] = np.concatenate([both((t - s) * 1.0 - P), both((t - s) * 1.0), both((t - s) * 1.0 + P)], 1)
    odc = np.concatenate([np.cos(ang), np.sin(ang), decay.transpose(1, 0, 2).reshape(P, -1)], 1).astype(np.float32)
    return con, pmask, sel, odc


def _layout(v):
    def cols(w):
        return np.asarray(w).reshape(-1, P).T

    def slots(w, kh, tiles):
        k, m = w.shape
        w = w.reshape(kh, k // P // kh, P, m // P, P).transpose(3, 0, 2, 1, 4)[tiles]
        return w.reshape(len(tiles) * kh, P, -1)

    v = {k: np.asarray(w) for k, w in v.items()}
    x_in = np.concatenate([v["x_prompt"][0], v["x_sample"][0]], 0).T.reshape(KD, P, T)
    ffn = [(v["ffn_a_w_in"][0], v["ffn_a_w_out"][0]), (v["ffn_b_w_in"][0], v["ffn_b_w_out"][0]),
           (v["ffn_a_w_in"][1], v["ffn_a_w_out"][1]), (v["ffn_b_w_in"][1], v["ffn_b_w_out"][1])]
    pairs = [t for j in range(FT) for t in (j, FT + j)]
    ev = list(range(2 * KD)) + [t for j in range(KD) for t in (2 * KD + j, 3 * KD + j)]
    od = [t for h in range(HG) for t in (h, KD + h, 2 * KD + h, 3 * KD + h, 4 * KD + h)]
    od += [(5 + part) * KD + HT * r + z for r in range(NH) for part in range(4) for z in range(HT)]
    every = list(range(KD))
    con, pmask, sel, odc = _host_constants()
    vec = np.concatenate([cols(v[n]) for n in (
        "ln_g", "ln_b", "ml_conv_w", "ml_conv_b", "ml_norm_g", "lru_conv_w", "lru_conv_b", "lru_b_a", "lru_b_x",
        "lru_lambda", "hg_lb_logits", "hg_norm_g", "ret_norm_g")], 1)
    w4 = np.stack([v[n].reshape(KD, P, 4) for n in ("ml_wq", "ml_wk", "ml_wv")]).transpose(2, 0, 1, 3)
    wg = np.stack([v["ml_w_ig"][0, 0], v["ml_w_fg"][0, 0], v["ml_w_ig"][0, 1], v["ml_w_fg"][0, 1]], 1)
    gb = np.stack([v["ml_b_ig"][0, 0], v["ml_b_fg"][0, 0], v["ml_b_ig"][0, 1], v["ml_b_fg"][0, 1]], 1)
    lru = np.stack([v["lru_w_a"][0, 0], v["lru_w_a"][0, 1], v["lru_w_x"][0, 0], v["lru_w_x"][0, 1]], 2)
    out = {
        "x_in": x_in, "con": con, "vec": vec, "pmask": pmask, "sel": sel, "odc": odc, "w4": w4,
        "wg": wg.reshape(3 * KD, P, 4, NH).transpose(1, 0, 2, 3), "gb": gb, "w_lru": lru,
        "w_in": np.concatenate([slots(w, 1, pairs) for w, _ in ffn]),
        "w_out": np.concatenate([slots(w, 2, every) for _, w in ffn]),
        "w_ev": slots(v["ev_w_in"][0], 1, ev), "w_evo": slots(v["ev_w_out"][0], 2, every),
        "w_od": slots(v["od_w_in"][0], 1, od), "w_odo": slots(v["od_w_out"][0], 2, every),
    }
    return {k: np.ascontiguousarray(w) for k, w in out.items()}


def kernel(**inputs):
    import concourse.bacc as bacc
    from concourse.bass_utils import run_bass_kernel_spmd

    arrays = _layout(inputs)
    nc = bacc.Bacc("TRN2", target_bir_lowering=False, num_devices=1)
    aps = {k: nc.dram_tensor(k, w.shape, mybir.dt.from_np(w.dtype), kind="ExternalInput").ap()
           for k, w in arrays.items()}
    aps["out"] = nc.dram_tensor("out", (KD, P, T), F32, kind="ExternalOutput").ap()
    build(nc, aps)
    r = run_bass_kernel_spmd(nc, [arrays], core_ids=[0])
    y = r.results[0]["out"].reshape(D, SEQS, L).transpose(1, 2, 0)
    return np.ascontiguousarray(y[0:1]), np.ascontiguousarray(y[1:2])
```

```python
from contextlib import ExitStack

import concourse.bass as bass
import numpy as np
from concourse import mybir

F32 = mybir.dt.float32
F32R = mybir.dt.float32r
U8 = mybir.dt.uint8
ALU = mybir.AluOpType
ACT = mybir.ActivationFunctionType

P = 128
SEQS, L = 2, 256
T = SEQS * L
SB = L // P
NB = SEQS * SB
D = 1024
KD = D // P
FF = 2816
FT = FF // P
KH = FT // 2
DEPTH = 2
ALPHA = (2.0 * DEPTH) ** 0.25
EPS = 1e-5
IN_SLOTS, OUT_SLOTS = 2 * FT, 2 * KD
EV_SLOTS, OD_SLOTS = 4 * KD, 9 * KD
NH = 4
HT = 2
HG = 8
LEVELS = 7
BY_ACT = (0, 1, 3, 4, 6, 7)
LOW_DVE = (0, 3, 6)
POOL_SUBS = 2
PAD = 3
AHEAD = (1, 3, 4, 6)

VEC = {}
for _name, _n in (("ln_g", 6 * KD), ("ln_b", 6 * KD), ("ml_cw", 4 * KD), ("ml_cb", KD), ("ml_g", KD),
                  ("lru_cw", 4 * KD), ("lru_cb", KD), ("b_a", 2 * KD), ("b_x", 2 * KD), ("lam", 2 * KD),
                  ("lb", 2 * KD), ("hg_g", KD), ("ret_g", KD)):
    VEC[_name] = sum(n for _, n in VEC.values()), _n
NV = sum(n for _, n in VEC.values())
CON = {}
for _name, _n in (("ident", P), ("mean_d", P), ("mean_256", P), ("mean_128", P), ("ones", P),
                  ("tri", 2 * L), ("bd", 32)):
    CON[_name] = sum(n for _, n in CON.values()), _n
NC = sum(n for _, n in CON.values())
NO = 2 * L + NH * 3 * P


def build(nc, a):
    off = [(nc.sbuf_base + 63) // 64 * 64]

    def at(name, shape, dt, where):
        return nc.alloc_sbuf_tensor_at(name, shape, dt, offset=where)

    def size(shape, dt):
        n = 1
        for s in shape[1:]:
            n *= s
        return (n * (1 if dt == U8 else 4) + 31) // 32 * 32

    def sb(name, shape, dt=F32, area=off):
        t = at("sb_" + name, shape, dt, area[0])
        area[0] += size(shape, dt)
        assert area[0] <= nc.sbuf_usable_end, (name, area[0], nc.sbuf_usable_end)
        return t

    x = sb("x", [P, KD, T])
    xh = sb("xh", [P, KD, T], F32R)
    xl = sb("xl", [P, KD, T], F32R)
    raw = sb("raw", [P, 2, KH * P])
    wh = sb("wh", [P, 2, KH * P], F32R)
    wl = sb("wl", [P, 2, KH * P], F32R)
    con = sb("con", [P, NC])
    vec = sb("vec", [P, NV])
    pmask = sb("pmask", [P, LEVELS, P], U8)
    w4 = sb("w4", [P, 3, KD, 4])
    wg = sb("wg", [P, 3 * KD, 4, NH])
    gb = sb("gb", [NH, 4])
    sel = sb("sel", [NH, NH, P])
    sp = sb("sp", [P, 3, 2 * KD])
    hbias = sb("hbias", [P, 4 * KD])
    lb = sb("lb", [P, 3, KD])
    gT = sb("gT", [P, 2, NB, NH])
    odd_area = [off[0]]
    odc = sb("odc", [P, NO], F32, odd_area)
    ev_area = [off[0]]
    negM = sb("negM", [NH, 2, T], F32, ev_area)
    thr = sb("thr", [NH, 2, T], F32, ev_area)
    free = max(odd_area[0], ev_area[0])

    fa = [free]
    hh = sb("hh", [P, FT, T], F32R, fa)
    hl = sb("hl", [P, FT, T], F32R, fa)
    sg = sb("sg", [P, 2, T], F32, fa)
    hf = sb("hf", [P, 2, T], F32, fa)
    lt = at("sb_lt", [P, 4, T], F32, fa[0] - 4 * T * 4)
    mask_f = at("sb_mask_f", [P, LEVELS, P], F32, fa[0] - LEVELS * P * 4)
    ma = [free]
    yhA = sb("yhA", [P, KD, T], F32R, ma)
    ylA = sb("ylA", [P, KD, T], F32R, ma)
    yB = ma[0]
    yhB = sb("yhB", [P, KD, T], F32R, ma)
    ylB = sb("ylB", [P, KD, T], F32R, ma)
    qk_area = [yB]
    q_all = sb("q_all", [P, KD, T], F32, qk_area)
    k_all = sb("k_all", [P, KD, T], F32, qk_area)
    tmp = ma[0]
    va = [tmp]
    vT = sb("vT", [P, NB, D], F32, va)
    e1 = [va[0]]
    um = sb("um", [P, 2, SEQS, L + PAD + 1], F32, e1)
    cv = sb("cv", [P, SEQS, L], F32, e1)
    cc = sb("cc", [P, 2, T], F32, e1)
    vf = sb("vf", [P, 2, T], F32, e1)
    bd = sb("bd", [P, 3, P], F32, e1)
    gtok = sb("gtok", [P, NB, 4, NH], F32, e1)
    e2 = [va[0]]
    gi = sb("gi", [NH, 2, T], F32, e2)
    gf = sb("gf", [NH, 2, T], F32, e2)
    g1 = sb("g1", [NH, 2, T], F32, e2)
    g2 = sb("g2", [NH, 2, T], F32, e2)
    one = sb("one", [NH, L], F32, e2)
    e3 = [va[0]]
    Ef = sb("Ef", [P, SEQS, L + P], F32, e3)
    Eb = sb("Eb", [P, SEQS, L + P], F32, e3)
    att = sb("att", [P, SEQS, SB, L], F32, e3)
    rec = sb("rec", [P, 2, T], F32, e3)
    hv = sb("hv", [P, HT, T], F32, e3)
    zs = sb("zs", [P, HT, T], F32, e3)
    dab = sb("dab", [P, T], F32, e3)
    rs = sb("rs", [P, T], F32, e3)
    ea = [tmp]
    lbd = sb("lbd", [P, 2, 4, P], F32, ea)
    lum = sb("lum", [P, SEQS, L + PAD + 1], F32, ea)
    lx = sb("lx", [P, SEQS, L], F32, ea)
    th = sb("th", [P, 2, 2, T], F32, ea)
    la = sb("la", [P, 2, T], F32, ea)
    lw = sb("lw", [P, 2, T], F32, ea)
    lr = sb("lr", [P, 2, T], F32, ea)
    lq = sb("lq", [P, 2, T], F32, ea)
    lix = sb("lix", [P, 2, T], F32, ea)
    lgl = sb("lgl", [P, T], F32, ea)
    ha, hy = [tmp], [yB]
    hq = sb("hq", [P, T], F32, ha)
    TA = sb("TA", [P, 3, T], F32, ha)
    TB = sb("TB", [P, 3, T // 2], F32, ha)
    Lo = sb("Lo", [P, 2, T], F32, ha)
    Up = sb("Up", [P, 2, T], F32, ha)
    KQ = sb("KQ", [P, 2, 2, T], F32, hy)
    ks = sb("ks", [P, T], F32, ha)
    hat = sb("hat", [P, 2, NB, P], F32, ha)
    hi_ = sb("hi_", [P, T], F32, ha)
    hvt = sb("hvt", [P, NB, P], F32, hy)
    hgs = sb("hgs", [P, 2, T], F32, ha)
    ho = sb("ho", [P, T], F32, ha)
    hsq = sb("hsq", [P, T], F32, hy)
    hrs = sb("hrs", [P, T], F32, hy)
    ra = [tmp]
    rq = sb("rq", [P, HT, T], F32, ra)
    rk = sb("rk", [P, HT, T], F32, ra)
    rt = sb("rt", [P, 4, T], F32, ra)
    rv = sb("rv", [P, T], F32, ra)
    rvt = sb("rvt", [P, NB, HT, P], F32, ra)
    ratt = sb("ratt", [P, SEQS, SB, L], F32, ra)
    rhv = sb("rhv", [P, HT, T], F32, ra)
    rzs = sb("rzs", [P, HT, T], F32, ra)
    rrec = sb("rrec", [P, T], F32, ra)

    def cn(name):
        o, n = CON[name]
        return con[:, o:o + n]

    def vc(name, i, n=1):
        return vec[:, bass.ds(VEC[name][0] + i, n)]

    ident, tri = cn("ident"), cn("tri")
    cos, sin = odc[:, 0:L], odc[:, L:2 * L]

    def seqs(ap):
        return ap.rearrange("p (s t) -> p s t", s=SEQS)

    def blocks(ap):
        return ap.rearrange("p (b t) -> p b t", b=NB)

    def halves(ap, B):
        v = ap.rearrange("p r (n two b) -> p r n two b", two=2, b=B)
        return v[:, :, :, 0, :], v[:, :, :, 1, :]

    def spread(ap, B):
        return ap[:, :, :, None].to_broadcast([P, 2, T // (2 * B), B])

    with ExitStack() as ctx:
        ps = ctx.enter_context(nc.psum_tensor("ps", [P, 8, T], F32))

        def sem(name):
            return ctx.enter_context(nc.semaphore("s_" + name))

        const_in, odd_in, x_in, out_done = sem("const_in"), sem("odd_in"), sem("x_in"), sem("out_done")
        raw_in, bd_in = [sem("raw_in0"), sem("raw_in1")], [sem("bd_in0"), sem("bd_in1")]
        hi_done, lo_done, w_used = sem("hi_done"), sem("lo_done"), sem("w_used")
        prep_d, prep_a = sem("prep_d"), sem("prep_a")
        step_done = sem("step_done")
        y_done, mean_mm, sum_done, sq_done = sem("y_done"), sem("mean_mm"), sem("sum_done"), sem("sq_done")
        var_mm, var_in, rstd_done = sem("var_mm"), sem("var_in"), sem("rstd_done")
        msq_done, m_done, sub_done = sem("msq_done"), sem("m_done"), sem("sub_done")
        x_dve, x_act, xh_done, xl_pool, xl_dve = (sem(n) for n in ("x_dve", "x_act", "xh_done", "xl_pool", "xl_dve"))
        scaled = sem("scaled")
        silu_done, glu_done, h_done = sem("silu_done"), sem("glu_done"), sem("h_done")
        um_zero, u_ev, c_lin, c_done, bd_done = sem("um_zero"), sem("u_ev"), sem("c_lin"), sem("c_done"), sem("bd_done")
        q_mm, k_mm, v_mm, q_ev, k_ev, v_ev = (sem(n) for n in ("q_mm", "k_mm", "v_mm", "q_ev", "k_ev", "v_ev"))
        vt_mm, vt_ev, gates_mm, gtok_ev, rows_mm = (sem(n) for n in ("vt_mm", "vt_ev", "gates_mm", "gtok_ev", "rows_mm"))
        rows_a, g_done, marg_done, thr_done, gT_mm, gT_ev = (
            sem(n) for n in ("rows_a", "g_done", "marg_done", "thr_done", "gT_mm", "gT_ev"))
        mb_mm, tb_mm, tb_ev, qk_mm, t_done, e_done, s_done = (
            sem(n) for n in ("mb_mm", "tb_mm", "tb_ev", "qk_mm", "t_done", "e_done", "s_done"))
        den_mm, abs_done, dmax_done, att_done, z_done = (
            sem(n) for n in ("den_mm", "abs_done", "dmax_done", "att_done", "z_done"))
        pv_mm, hv_done, hmean_mm, hcen_done, hsq_done = (
            sem(n) for n in ("pv_mm", "hv_done", "hmean_mm", "hcen_done", "hsq_done"))
        hvar_mm, hvar_in, hrstd_done = sem("hvar_mm"), sem("hvar_in"), sem("hrstd_done")
        mix_done = sem("mix_done")
        lzero, lu_ev, lx_done, lg_mm, gelu_done, lt_done = (
            sem(n) for n in ("lzero", "lu_ev", "lx_done", "lg_mm", "gelu_done", "lt_done"))
        la_done, lw_done, lsq_done, lix_done = (
            sem(n) for n in ("la_done", "lw_done", "lsq_done", "lix_done"))
        a_sig, a_i, a_q, a_kq, a_g, a_vt_mm, a_vt = (
            sem(n) for n in ("a_sig", "a_i", "a_q", "a_kq", "a_g", "a_vt_mm", "a_vt"))
        a_diag_mm, a_diag, a_cp, a_lv_mm, a_up, a_pred = (
            sem(n) for n in ("a_diag_mm", "a_diag", "a_cp", "a_lv_mm", "a_up", "a_pred"))
        a_off_mm, a_off, a_pv, a_sq, a_var, a_vin, a_rstd = (
            sem(n) for n in ("a_off_mm", "a_off", "a_pv", "a_sq", "a_var", "a_vin", "a_rstd"))
        r_q, r_k, rv_ev, rvt_mm, rvt_ev, rqk_mm, ratt_done, rz_ev, rz_done = (
            sem(n) for n in ("r_q", "r_k", "rv_ev", "rvt_mm", "rvt_ev", "rqk_mm", "ratt_done", "rz_ev", "rz_done"))

        kinds = ["ffn", "even", "ffn", "ffn", "odd", "ffn"]
        own = {"ffn": IN_SLOTS, "even": EV_SLOTS, "odd": OD_SLOTS}
        stages = []
        for kind in kinds:
            n0 = sum(own[k] + OUT_SLOTS for k, _, _ in stages)
            stages.append((kind, n0, sum(k == "ffn" for k, _, _ in stages)))
        MIX_EVEN, MIX_ODD = NH + KD, HG + NH

        class Slot:

            def __init__(self, n0, i, per, j):
                self.half, self.par = n0 // 2 + (per // 2) * i + j // 2, j % 2
                self.n = 2 * self.half + self.par

        block = ctx.enter_context(nc.Block())

        @block.sync
        def _(sync):
            def load(src, kt, sl):
                sync.wait_ge(hi_done, sl.n + 1)
                sync.wait_ge(lo_done, sl.n + 1)
                sync.dma_start(raw[:, sl.par, 0:kt * P], src).then_inc(raw_in[sl.par], 16)

            def stream(w, first, n, kt, n0, begun=False):
                if begun:
                    load(slot_of(w, first + 1), kt, Slot(n0, 0, 2, 1))
                with sync.Fori(int(begun), n // 2) as i:
                    for j in range(2):
                        load(slot_of(w, first + 2 * i + j), kt, Slot(n0, i, 2, j))

            def slot_of(w, n):
                return w[bass.ds(n, 1), :, :].rearrange("a p c -> (a p) c")

            load(slot_of(a["w_in"], 0), KD, Slot(0, 0, 2, 0))
            sync.dma_start(x[:], a["x_in"].rearrange("k p t -> p k t")).then_inc(x_in, 16)
            for kind, n0, fi in stages:
                if kind == "ffn":
                    stream(a["w_in"], fi * IN_SLOTS, IN_SLOTS, KD, n0, begun=n0 == 0)
                    stream(a["w_out"], fi * OUT_SLOTS, OUT_SLOTS, KH, n0 + IN_SLOTS)
                elif kind == "even":
                    stream(a["w_ev"], 0, 2 * KD, KD, n0)
                    with sync.Fori(0, KD // 2) as i:
                        for j in range(2):
                            for h in range(2):
                                load(slot_of(a["w_ev"], 2 * KD + 4 * i + 2 * j + h), KD,
                                     Slot(n0 + 2 * KD, i, 4, 2 * j + h))
                            sync.wait_ge(lzero, 1)
                            sync.wait_ge(lg_mm, 8 * i + 1)
                            for b in range(2):
                                sync.dma_start(
                                    lbd[64 * b:64 * b + 64, j, :, 64 * b:64 * b + 64],
                                    a["w_lru"][bass.ds(4 * i + 2 * j + b, 1), :, :, :].rearrange(
                                        "a c g d -> (a c) g d")).then_inc(bd_in[j], 16)
                    stream(a["w_evo"], 0, OUT_SLOTS, KD, n0 + EV_SLOTS)
                else:
                    sync.wait_ge(mix_done, MIX_EVEN)
                    sync.dma_start(odc[:], a["odc"]).then_inc(odd_in, 16)
                    stream(a["w_od"], 0, OD_SLOTS, KD, n0)
                    stream(a["w_odo"], 0, OUT_SLOTS, KD, n0 + OD_SLOTS)
            sync.wait_ge(x_dve, (KD - len(BY_ACT)) * len(stages))
            sync.wait_ge(x_act, len(BY_ACT) * len(stages))
            sync.dma_start(a["out"].rearrange("k p t -> p k t"), x[:]).then_inc(out_done, 16)
            sync.wait_ge(out_done, 16)

        @block.gpsimd
        def _(pool):
            pool.sem_inc(lo_done, 2)
            for t, name in ((con, "con"), (vec, "vec"), (mask_f, "pmask"), (w4, "w4"), (wg, "wg"), (gb, "gb"), (sel, "sel")):
                pool.dma_start(t[:], a[name]).then_inc(const_in, 16)

            def lo(kt, sl):
                pool.wait_ge(hi_done, sl.n + 3)
                n = kt * P
                pool.tensor_tensor(wl[:, sl.par, 0:n], raw[:, sl.par, 0:n], wh[:, sl.par, 0:n].bitcast(F32),
                                   ALU.subtract).then_inc(lo_done, 1)

            def los(n, kt, n0, last, begun=False):
                if begun:
                    lo(kt, Slot(n0, 0, 2, 2))
                with pool.Fori(int(begun), n // 2 - 1) as i:
                    for j in range(1, 3):
                        lo(kt, Slot(n0, i, 2, j))
                lo(kt, Slot(n0, n // 2 - 1, 2, 1))
                if last:
                    lo(last, Slot(n0, n // 2 - 1, 2, 2))

            def low_of_x(n):
                for k in range(KD):
                    if k not in LOW_DVE:
                        pool.wait_ge(xh_done, KD * n + k + 1)
                        pool.tensor_tensor(xl[:, k, :], x[:, k, :], xh[:, k, :].bitcast(F32),
                                           ALU.subtract).then_inc(xl_pool, 1)

            lo(KD, Slot(0, 0, 2, 0))
            pool.wait_ge(x_in, 16)
            low_of_x(0)
            lo(KD, Slot(0, 0, 2, 1))

            for st, (kind, n0, fi) in enumerate(stages):
                more = st < len(stages) - 1
                if kind == "ffn":
                    los(IN_SLOTS, KD, n0, KH, begun=True)
                    los(OUT_SLOTS, KH, n0 + IN_SLOTS, KD if more else 0)
                elif kind == "even":
                    los(2 * KD, KD, n0, KD, begun=True)
                    los(2 * KD, KD, n0 + 2 * KD, KD)
                    los(OUT_SLOTS, KD, n0 + EV_SLOTS, KD if more else 0)
                else:
                    los(OD_SLOTS, KD, n0, KD, begun=True)
                    los(OUT_SLOTS, KD, n0 + OD_SLOTS, KD if more else 0)
                pool.wait_ge(m_done, st + 1)
                pool.wait_ge(sq_done, (KD - 1) * (st + 1))
                for k in range(KD - POOL_SUBS, KD):
                    pool.tensor_tensor(x[:, k, :], x[:, k, :], lt[:, 0, :], ALU.subtract).then_inc(sub_done, 1)
                if more:
                    lo(KD, Slot(stages[st + 1][1], 0, 2, 1))
                    low_of_x(st + 1)

        @block.tensor
        def _(pe):
            pe.sem_inc(w_used, 2)
            for s in (lg_mm, rvt_mm, a_pv, a_diag_mm):
                pe.sem_inc(s, 1)

            def proj(bank, kt, sl, rh, rl, start=True, stop=True):
                pe.wait_ge(hi_done, sl.n + 3)
                pe.wait_ge(lo_done, sl.n + 3)
                out = ps[:, bank, :]
                for k in range(kt):
                    w_h, w_l = (w[:, sl.par, k * P:k * P + P] for w in (wh, wl))
                    pe.matmul(out, w_l, rh(k), start=start and k == 0, stop=False)
                    pe.matmul(out, w_h, rl(k), start=False, stop=False)
                    mm = pe.matmul(out, w_h, rh(k), start=False, stop=stop and k == kt - 1)
                mm.then_inc(w_used, 1)

            def of_x(bank, sl, fresh=None):
                def x_l(k):
                    return xl[:, k, :]

                def x_h(k):
                    if fresh is not None:
                        s, n = (xl_dve, LOW_DVE) if k in LOW_DVE else (xl_pool, tuple(set(range(KD)) - set(LOW_DVE)))
                        pe.wait_ge(s, len(n) * fresh + sum(m <= k for m in n))
                    return xh[:, k, :]

                proj(bank, KD, sl, x_h, x_l)

            def ffn_in(fi, n0, st):
                with pe.Fori(0, FT // 2) as i:
                    for b in range(2):
                        pe.wait_ge(glu_done, FT * fi + 2 * i + b + 1)
                        of_x(2 * b, Slot(n0, i, 4, 2 * b), st if b == 0 else None)
                        of_x(2 * b + 1, Slot(n0, i, 4, 2 * b + 1))

            def out_phase(ln, n0, kt, parts, second_half):
                def tiles(i, first=False):
                    for b in range(2):
                        pe.wait_ge(y_done, KD * ln + 2 * i + b + 1)
                        for kh, (rh, rl) in enumerate(parts):
                            if first and b == 0 and kh == 1:
                                pe.wait_ge(*second_half)
                            proj(4 + b, kt, Slot(n0, i, 4, 2 * b + kh), rh, rl, start=kh == 0, stop=kh == 1)

                tiles(0, first=True)
                for k in range(2):
                    pe.wait_ge(y_done, KD * ln + k + 3)
                    mm = pe.matmul(ps[:, 6, :], cn("mean_256"), x[:, k, :], start=k == 0, stop=k == 1)
                mm.then_inc(mean_mm, 1)
                with pe.Fori(1, KD // 2) as i:
                    tiles(i)
                pe.wait_ge(sum_done, (KD - 1) * (ln + 1))
                pe.matmul(ps[:, 6, :], cn("mean_d"), lt[:, 0, :], start=True, stop=True).then_inc(mean_mm, 1)
                pe.wait_ge(sq_done, (KD - 1) * (ln + 1))
                pe.matmul(ps[:, 7, :], cn("mean_d"), lt[:, 1, :], start=True, stop=True).then_inc(var_mm, 1)

            def head_mean(c, bank, src, banked):
                pe.wait_ge(hv_done, c + 1)
                banked()
                for z in range(HT):
                    mm = pe.matmul(ps[:, bank, :], cn("mean_256"), src[:, z, :], start=z == 0, stop=z == HT - 1)
                mm.then_inc(hmean_mm, 1)

            def head_var(c, bank, src):
                pe.wait_ge(hsq_done, c + 1)
                for z in range(HT):
                    mm = pe.matmul(ps[:, bank, :], cn("mean_256"), src(z), start=z == 0, stop=z == HT - 1)
                mm.then_inc(hvar_mm, 1)

            def even(n0, st):
                for t in range(KD + 2):
                    if t < KD:
                        if t >= 2:
                            pe.wait_ge(u_ev, t - 1)
                        of_x(t % 2, Slot(n0, 0, 2, t), st if t == 0 else None)
                    if t >= 2:
                        m = t - 2
                        pe.wait_ge(q_ev, m + 1)
                        pe.wait_ge(k_ev, m + 1)
                        pe.wait_ge(v_ev, m + 1)
                        for part, src in enumerate((q_all[:, m, :], k_all[:, m, :], vf[:, m % 2, :])):
                            for b in range(NB):
                                first, last = m == 0 and part == 0 and b == 0, m == KD - 1 and part == 2
                                mm = pe.matmul(ps[:, 6, b * 4 * NH:(b + 1) * 4 * NH], src[:, b * P:(b + 1) * P],
                                               wg[:, part * KD + m, :, :].rearrange("p y h -> p (y h)"),
                                               start=first, stop=last, skip_group_check=True)
                        if m == KD - 1:
                            mm.then_inc(gates_mm, 1)
                        if m >= 1:
                            pe.wait_ge(vt_ev, m)
                        for b in range(NB):
                            mm = pe.transpose(ps[:, 5, b * P:(b + 1) * P], vf[:, m % 2, b * P:(b + 1) * P], ident)
                        mm.then_inc(vt_mm, 1)
                    if 1 <= t <= KD:
                        m = t - 1
                        pe.wait_ge(bd_done, m + 1)
                        pe.wait_ge(c_done, m + 1)
                        if m >= 1:
                            pe.wait_ge(q_ev, m)
                        pe.matmul(ps[:, 2, :], bd[:, 0, :], cc[:, m % 2, :], start=True, stop=True).then_inc(q_mm, 1)
                        if m >= 1:
                            pe.wait_ge(k_ev, m)
                        pe.matmul(ps[:, 3, :], bd[:, 1, :], cc[:, m % 2, :], start=True, stop=True).then_inc(k_mm, 1)
                        if m >= 1:
                            pe.wait_ge(v_ev, m)
                        pe.matmul(ps[:, 4, :], bd[:, 2, :], um[:, m % 2, :, 2:2 + L], start=True,
                                  stop=True).then_inc(v_mm, 1)
                pe.wait_ge(gtok_ev, 1)
                for y in range(4):
                    for b in range(NB):
                        mm = pe.transpose(ps[0:NH, y, b * P:(b + 1) * P], gtok[:, b, y, :], ident)
                    mm.then_inc(rows_mm, 1)
                pe.wait_ge(g_done, 1)
                for d in range(2):
                    for b in range(NB):
                        o = (d * NB + b) * NH
                        mm = pe.transpose(ps[:, 4, o:o + NH], gi[:, d, b * P:(b + 1) * P], ident[0:NH, 0:NH])
                mm.then_inc(gT_mm, 1)

                def keys_queries(h):
                    if h >= 1:
                        pe.wait_ge(s_done, 2 * h)
                    for q in range(SEQS):
                        for sb_ in range(SB):
                            for z in range(HT):
                                o = q * L + sb_ * P
                                mm = pe.matmul(ps[:, 6 + q, sb_ * L:(sb_ + 1) * L], k_all[:, HT * h + z, o:o + P],
                                               q_all[:, HT * h + z, q * L:(q + 1) * L],
                                               start=z == 0, stop=z == HT - 1)
                    mm.then_inc(qk_mm, 1)

                keys_queries(0)
                pe.wait_ge(thr_done, 1)
                pe.wait_ge(gT_ev, 1)
                for h in range(NH):
                    if h >= 1:
                        pe.wait_ge(hv_done, h)
                    for d in range(2):
                        pe.matmul(ps[:, 2 + d, :], sel[:, h, :], negM[:, d, :], start=True, stop=True).then_inc(mb_mm, 1)
                    if h >= 1:
                        pe.wait_ge(abs_done, 2 * h)
                    if h >= 2:
                        pe.wait_ge(hvar_in, h - 1)
                    for d in range(2):
                        pe.matmul(ps[:, 4 + d, :], sel[:, h, :], thr[:, d, :], start=True, stop=True).then_inc(tb_mm, 1)
                    if h >= 1:
                        pe.wait_ge(z_done, HT * h)
                    of_x(0, Slot(n0, 0, 2, KD + HT * h))
                    if h >= 1:
                        head_mean(h - 1, 5, hv, lambda: pe.wait_ge(tb_ev, 2 * h + 2))
                    for d, E in enumerate((Ef, Eb)):
                        pe.wait_ge(s_done, 2 * h + d + 1)
                        if d == 0:
                            pe.wait_ge(tb_ev, 2 * h + 1)
                        else:
                            pe.wait_ge(abs_done, 2 * h + 1)
                        for q in range(SEQS):
                            pe.matmul(ps[:, 4, q * L:(q + 1) * L], cn("ones"), E[:, q, 0:L], start=True, stop=False)
                            o = q * L + (P if d == 0 else 0)
                            mm = pe.matmul(ps[:, 4, o:o + P], cn("ones"), E[:, q, L:L + P], start=False, stop=True)
                        mm.then_inc(den_mm, 1)
                    of_x(1, Slot(n0, 0, 2, KD + HT * h + 1))
                    if h >= 1:
                        head_var(h - 1, 5, lambda z: q_all[:, HT * (h - 1) + z, :])
                    if h < NH - 1:
                        keys_queries(h + 1)
                    pe.wait_ge(att_done, h + 1)
                    for z in range(HT):
                        for q in range(SEQS):
                            for sb_ in range(SB):
                                o = (HT * h + z) * P
                                mm = pe.matmul(ps[:, 2 + z, q * L:(q + 1) * L], vT[:, q * SB + sb_, o:o + P],
                                               att[:, q, sb_, :], start=sb_ == 0, stop=sb_ == SB - 1)
                    mm.then_inc(pv_mm, 1)
                pe.wait_ge(hvar_in, NH - 1)
                head_mean(NH - 1, 5, hv, lambda: None)
                head_var(NH - 1, 5, lambda z: q_all[:, HT * (NH - 1) + z, :])
                pe.wait_ge(z_done, HT * NH)

                n1 = n0 + 2 * KD

                def lru(i, j):
                    t = 2 * i + j
                    pe.wait_ge(lu_ev, t + 1)
                    of_x(0, Slot(n1, i, 4, 2 * j))
                    pe.wait_ge(gelu_done, t + 1)
                    of_x(1, Slot(n1, i, 4, 2 * j + 1))
                    pe.wait_ge(lx_done, t + 1)
                    pe.wait_ge(bd_in[j], 32 * (i + 1))
                    for g in range(4):
                        pe.wait_ge(lt_done, 4 * t + 1)
                        pe.matmul(ps[:, 2 + g, :], lbd[:, j, g, :], lx[:].rearrange("p s t -> p (s t)"),
                                  start=True, stop=True).then_inc(lg_mm, 1)

                with pe.Fori(0, KD // 2) as i:
                    lru(i, 0)
                    lru(i, 1)

            def odd(n0, st):
                hgrn_in = (0, 1, 2, 3, 4)
                for m in range(5):
                    of_x(m, Slot(n0, 0, 2, m), st if m == 0 else None)

                def front(h):
                    pe.wait_ge(a_i, h + 1)
                    for b_ in range(NB):
                        mm = pe.transpose(ps[:, 3, b_ * P:(b_ + 1) * P], hi_[:, b_ * P:(b_ + 1) * P], ident)
                    mm.then_inc(a_vt_mm, 1)

                def diag(h):
                    pe.wait_ge(a_kq, h + 1)
                    pe.wait_ge(a_off, h + 1)
                    for b_ in range(NB):
                        c = slice(b_ * P, (b_ + 1) * P)
                        mm = pe.matmul(ps[:, 5, c], ks[:, c], hq[:, c], start=True, stop=True)
                    mm.then_inc(a_diag_mm, 1)

                def mix(i, b, more):
                    h = 2 * i + b
                    read = [(a_q, h + 1), (a_sig, 4 * h + 2), (a_sig, 4 * h + 3), (a_vt, h + 1), (a_g, h + 1)]

                    def nxt(k):
                        pe.wait_ge(*read[k])
                        of_x(hgrn_in[k], Slot(n0, i, 10, 5 * b + 5 + k))

                    nxt(0)
                    diag(h)
                    for l in range(LEVELS):
                        pe.wait_ge(a_cp, LEVELS * h + l + 1)
                        if l == 0:
                            pe.wait_ge(a_vin, h + 1)
                        elif l == 1:
                            pe.wait_ge(a_diag, h + 1)
                        else:
                            pe.wait_ge(a_pred, LEVELS * h + l - 1)
                        for b_ in range(NB):
                            c = slice(b_ * P, (b_ + 1) * P)
                            mm = pe.matmul(ps[:, 6 - l % 2, c], KQ[:, l % 2, 0, c], KQ[:, l % 2, 1, c],
                                           start=True, stop=True)
                        mm.then_inc(a_lv_mm, 1)
                        if l in AHEAD:
                            nxt(AHEAD.index(l) + 1)
                    pe.wait_ge(a_up, LEVELS * h + LEVELS)
                    pe.wait_ge(a_pred, LEVELS * h + LEVELS - 1)
                    for q in range(SEQS):
                        c0, c1 = slice(q * L, q * L + P), slice(q * L + P, q * L + L)
                        pe.matmul(ps[:, 5, c0], Lo[:, 0, c0], Up[:, 1, c1], start=True, stop=True)
                        mm = pe.matmul(ps[:, 5, c1], Up[:, 0, c1], Lo[:, 1, c0], start=True, stop=True)
                    mm.then_inc(a_off_mm, 1)
                    pe.wait_ge(a_off, h + 2)
                    pe.wait_ge(a_pred, LEVELS * h + LEVELS)
                    pe.wait_ge(mix_done, MIX_EVEN + h)
                    for q in range(SEQS):
                        for tb in range(SB):
                            for sb_ in range(SB):
                                o = q * L + tb * P
                                mm = pe.matmul(ps[:, 7, o:o + P], hvt[:, q * SB + sb_, :],
                                               hat[:, int(sb_ != tb), q * SB + sb_, :], start=sb_ == 0, stop=sb_ == SB - 1)
                    mm.then_inc(a_pv, 1)
                    if more:
                        front(h + 1)
                    pe.wait_ge(a_sq, h + 1)
                    pe.matmul(ps[:, 6, :], cn("mean_128"), hsq[:], start=True, stop=True).then_inc(a_var, 1)

                front(0)
                with pe.Fori(0, HG // 2 - 1) as i:
                    mix(i, 0, True)
                    mix(i, 1, True)
                mix(HG // 2 - 1, 0, True)
                mix(HG // 2 - 1, 1, False)
                n1 = n0 + 5 * HG
                pe.wait_ge(mix_done, MIX_EVEN + HG)
                pe.wait_ge(a_vin, HG + 1)

                def ret(r, more):
                    c = NH + r

                    def slot(m, bank):
                        of_x(bank, Slot(n1, r, 8, m))

                    pe.wait_ge(r_q, r + 1)
                    slot(5, 0)
                    pe.wait_ge(r_k, r + 1)
                    pe.wait_ge(hvar_in, c)
                    for q in range(SEQS):
                        for sb_ in range(SB):
                            for z in range(HT):
                                o = q * L + sb_ * P
                                mm = pe.matmul(ps[:, 6 + q, sb_ * L:(sb_ + 1) * L], rk[:, z, o:o + P],
                                               rq[:, z, q * L:(q + 1) * L], start=z == 0, stop=z == HT - 1)
                    mm.then_inc(rqk_mm, 1)
                    slot(6, 1)
                    turn_v(r, 0)
                    slot(7, 2)
                    turn_v(r, 1)
                    pe.wait_ge(ratt_done, r + 1)
                    pe.wait_ge(rvt_ev, HT * r + HT + 1)
                    for z in range(HT):
                        for q in range(SEQS):
                            for sb_ in range(SB):
                                mm = pe.matmul(ps[:, 3 + z, q * L:(q + 1) * L], rvt[:, q * SB + sb_, z, :],
                                               ratt[:, q, sb_, :], start=sb_ == 0, stop=sb_ == SB - 1)
                    mm.then_inc(pv_mm, 1)
                    if more:
                        slot(8, 0)
                    head_mean(c, 6, rhv, lambda: None)
                    if more:
                        pe.wait_ge(rz_done, HT * r + 1)
                        slot(9, 1)
                    head_var(c, 7, lambda z: rq[:, z, :])
                    if more:
                        pe.wait_ge(rz_done, HT * r + 2)
                        slot(10, 2)
                        slot(11, 3)
                        slot(12, 4)

                def turn_v(r, z):
                    pe.wait_ge(rv_ev, HT * r + z + 1)
                    pe.wait_ge(rvt_ev, HT * r + z + 1)
                    for b_ in range(NB):
                        mm = pe.transpose(ps[:, 5, b_ * P:(b_ + 1) * P], rv[:, b_ * P:(b_ + 1) * P], ident)
                    mm.then_inc(rvt_mm, 1)

                with pe.Fori(0, NH - 1) as r:
                    ret(r, True)
                ret(NH - 1, False)

            mixed = 0
            for st, (kind, n0, fi) in enumerate(stages):
                if kind == "ffn":
                    ffn_in(fi, n0, st)
                    if st == 0:
                        pe.wait_ge(const_in, 16 * 7)
                    pe.wait_ge(h_done, FT * fi + KH)
                    out_phase(st, n0 + IN_SLOTS, KH, [
                        (lambda k: hh[:, k, :], lambda k: hl[:, k, :]),
                        (lambda k: hh[:, KH + k, :], lambda k: hl[:, KH + k, :])], (h_done, FT * (fi + 1)))
                else:
                    (even if kind == "even" else odd)(n0, st)
                    mixed += MIX_EVEN if kind == "even" else MIX_ODD
                    if kind == "even":
                        pe.wait_ge(mix_done, mixed - KD)
                        pe.wait_ge(lt_done, 4 * KD + 1)
                    else:
                        pe.wait_ge(mix_done, mixed - NH)
                        pe.wait_ge(hv_done, 2 * NH)
                    out_phase(st, n0 + own[kind], KD, [
                        (lambda k: yhA[:, k, :], lambda k: ylA[:, k, :]),
                        (lambda k: yhB[:, k, :], lambda k: ylB[:, k, :])], (mix_done, mixed))

        @block.scalar
        def _(act):
            def split(kt, sl):
                act.wait_ge(raw_in[sl.par], 16 * (sl.half + 1))
                act.wait_ge(w_used, sl.n + 1)
                act.activation(wh[:, sl.par, 0:kt * P], raw[:, sl.par, 0:kt * P], ACT.Copy).then_inc(hi_done, 1)

            def ln_and_exp():
                act.preload_act_table_set("natural_log_exp_and_others")

            def used(sl):
                act.wait_ge(w_used, sl.n + 3)

            def ffn(fi, n0, nxt):
                def tile(i, b, after, begun=False):
                    if not begun:
                        split(KD, Slot(n0, i, 4, 2 * b + 1))
                    split(after, Slot(n0, i, 4, 2 * b + 2))
                    used(Slot(n0, i, 4, 2 * b))
                    act.wait_ge(glu_done, FT * fi + 2 * i + b + 1)
                    act.activation(sg[:, b, :], ps[:, 2 * b, :], ACT.Silu).then_inc(silu_done, 1)

                tile(0, 0, KD, begun=True)
                tile(0, 1, KD)
                with act.Fori(1, FT // 2 - 1) as i:
                    tile(i, 0, KD)
                    tile(i, 1, KD)
                tile(FT // 2 - 1, 0, KD)
                tile(FT // 2 - 1, 1, KH)
                out_splits(n0 + IN_SLOTS, KH, nxt)

            def out_splits(n0, kt, nxt):
                with act.Fori(0, OUT_SLOTS // 2 - 1) as i:
                    split(kt, Slot(n0, i, 2, 1))
                    split(kt, Slot(n0, i, 2, 2))
                split(kt, Slot(n0, OUT_SLOTS // 2 - 1, 2, 1))
                if nxt:
                    split(KD, Slot(n0, OUT_SLOTS // 2 - 1, 2, 2))

            def layer_norm(ln):
                ln_and_exp()
                act.wait_ge(mean_mm, 2 * ln + 2)
                act.activation(lt[:, 0, :], ps[:, 6, :], ACT.Copy).then_inc(m_done, 1)
                act.wait_ge(sq_done, (KD - 1) * (ln + 1))
                act.wait_ge(m_done, ln + 1)
                act.activation(lt[:, 2, :], lt[:, 0, :], ACT.Square).then_inc(msq_done, 1)
                act.wait_ge(var_in, ln + 1)
                act.activation(lt[:, 1, :], lt[:, 3, :], ACT.Ln).then_inc(rstd_done, 1)
                act.wait_ge(rstd_done, 2 * ln + 1)
                act.activation(lt[:, 3, :], lt[:, 1, :], ACT.Exp, scale=-0.5).then_inc(rstd_done, 1)
                if ln < len(stages) - 1:
                    split(KD, Slot(stages[ln + 1][1], 0, 2, 1))
                for k in range(KD):
                    if k in BY_ACT:
                        act.wait_ge(scaled, KD * ln + k + 1)
                        act.activation(x[:, k, :], x[:, k, :], ACT.Identity, scale=vc("ln_g", ln * KD + k),
                                       bias=vc("ln_b", ln * KD + k)).then_inc(x_act, 1)
                    if ln < len(stages) - 1:
                        if k in BY_ACT:
                            act.wait_ge(x_act, len(BY_ACT) * ln + sum(m <= k for m in BY_ACT))
                        else:
                            act.wait_ge(x_dve, (KD - len(BY_ACT)) * ln + sum(m not in BY_ACT for m in range(k + 1)))
                        act.activation(xh[:, k, :], x[:, k, :], ACT.Copy).then_inc(xh_done, 1)

            def head_square(c, src, dst):
                act.wait_ge(hcen_done, c + 1)
                act.activation(dst, src[:], ACT.Square).then_inc(hsq_done, 1)

            def head_rstd(c, r):
                ln_and_exp()
                act.wait_ge(hvar_in, c + 1)
                act.activation(r, r, ACT.Ln).then_inc(hrstd_done, 1)
                act.wait_ge(hrstd_done, 2 * c + 1)
                act.activation(r, r, ACT.Exp, scale=-0.5).then_inc(hrstd_done, 1)

            def even(n0):
                for t in range(KD + 2):
                    if t < KD:
                        if t >= 1:
                            split(KD, Slot(n0, 0, 2, t + 1))
                        used(Slot(n0, 0, 2, t))
                        if t == 0:
                            act.wait_ge(um_zero, 1)
                        if t >= 2:
                            act.wait_ge(c_lin, t - 1)
                            act.wait_ge(v_mm, t - 1)
                        act.activation(um[:, t % 2, :, 2:2 + L], seqs(ps[:, t % 2, :]), ACT.Copy).then_inc(u_ev, 1)
                    if t >= 2:
                        m = t - 2
                        act.wait_ge(vt_mm, m + 1)
                        act.activation(vT[:, :, m * P:(m + 1) * P], blocks(ps[:, 5, :]), ACT.Copy).then_inc(vt_ev, 1)
                    if 1 <= t <= KD:
                        m = t - 1
                        act.wait_ge(q_mm, m + 1)
                        act.activation(q_all[:, m, :], ps[:, 2, :], ACT.Copy).then_inc(q_ev, 1)
                        act.wait_ge(k_mm, m + 1)
                        act.activation(k_all[:, m, :], ps[:, 3, :], ACT.Copy, scale=1.0 / 16.0).then_inc(k_ev, 1)
                        act.wait_ge(v_mm, m + 1)
                        act.activation(vf[:, m % 2, :], ps[:, 4, :], ACT.Copy).then_inc(v_ev, 1)
                    if t < KD:
                        act.wait_ge(c_lin, t + 1)
                        act.activation(seqs(cc[:, t % 2, :]), cv[:], ACT.Silu, bias=vc("ml_cb", t)).then_inc(c_done, 1)
                act.wait_ge(gates_mm, 1)
                act.activation(gtok[:].rearrange("p b y h -> p (b y h)"), ps[:, 6, 0:NB * 4 * NH],
                               ACT.Copy).then_inc(gtok_ev, 1)
                ln_and_exp()
                for d in range(2):
                    act.wait_ge(rows_mm, 2 * d + 2)
                    act.activation(gi[:, d, :], ps[0:NH, 2 * d, :], ACT.Identity,
                                   bias=gb[:, 2 * d:2 * d + 1]).then_inc(rows_a, 1)
                    act.activation(gf[:, d, :], ps[0:NH, 2 * d + 1, :], ACT.Identity,
                                   bias=gb[:, 2 * d + 1:2 * d + 2]).then_inc(rows_a, 1)
                act.wait_ge(rows_a, 4)
                act.activation(g1[:], gf[:], ACT.Abs).then_inc(rows_a, 1)
                act.wait_ge(rows_a, 5)
                act.activation(g1[:], g1[:], ACT.Exp, scale=-1.0).then_inc(rows_a, 1)
                act.wait_ge(rows_a, 6)
                act.activation(g2[:], g1[:], ACT.Ln, bias=1.0).then_inc(rows_a, 1)
                act.wait_ge(gT_mm, 1)
                act.activation(gT[:].rearrange("p d b h -> p (d b h)"), ps[:, 4, 0:2 * NB * NH],
                               ACT.Copy).then_inc(gT_ev, 1)
                act.wait_ge(marg_done, 1)
                act.activation(thr[:], g1[:], ACT.Exp).then_inc(thr_done, 1)
                for h in range(NH):
                    for d in range(2):
                        act.wait_ge(tb_mm, 2 * h + d + 1)
                        if h >= 1:
                            act.wait_ge(att_done, h)
                        act.activation(rec[:, d, :], ps[:, 4 + d, :], ACT.Copy).then_inc(tb_ev, 1)
                    for d, E in enumerate((Ef, Eb)):
                        act.wait_ge(t_done, 2 * h + d + 1)
                        act.activation(E[:], E[:], ACT.Exp).then_inc(e_done, 1)
                    split(KD, Slot(n0, 0, 2, KD + HT * h + 1))
                    if h >= 1:
                        head_square(h - 1, hv, q_all[:, HT * (h - 1):HT * h, :])
                    for d in range(2):
                        act.wait_ge(den_mm, 2 * h + d + 1)
                        if h + d:
                            act.wait_ge(dmax_done, 2 * h + d)
                        act.activation(dab[:], ps[:, 4, :], ACT.Abs).then_inc(abs_done, 1)
                    split(KD, Slot(n0, 0, 2, KD + HT * h + 2))
                    if h >= 1:
                        head_rstd(h - 1, rs[:])
                    if h >= 1:
                        act.wait_ge(mix_done, h)
                    for z in range(HT):
                        used(Slot(n0, 0, 2, KD + HT * h + z))
                        act.activation(zs[:, z, :], ps[:, z, :], ACT.Sigmoid).then_inc(z_done, 1)
                    act.wait_ge(pv_mm, h + 1)
                    act.activation(hv[:], ps[:, 2:4, :], ACT.Copy).then_inc(hv_done, 1)
                head_square(NH - 1, hv, q_all[:, HT * (NH - 1):HT * NH, :])
                head_rstd(NH - 1, rs[:])

                n1 = n0 + 2 * KD
                act.wait_ge(lzero, 1)

                def u(i, j):
                    split(KD, Slot(n1, i, 4, 2 * j + 1))
                    used(Slot(n1, i, 4, 2 * j))
                    act.activation(lum[:, :, 2:2 + L], seqs(ps[:, 0, :]), ACT.Copy).then_inc(lu_ev, 1)

                def lru(i, j, more):
                    t = 2 * i + j
                    split(KD, Slot(n1, i, 4, 2 * j + 2))
                    used(Slot(n1, i, 4, 2 * j + 1))
                    act.wait_ge(mix_done, NH + t)
                    act.activation(lgl[:], ps[:, 1, :], ACT.Gelu_apprx_tanh).then_inc(gelu_done, 1)
                    act.wait_ge(lix_done, t + 1)
                    for g in range(2):
                        for d in range(2):
                            act.wait_ge(lg_mm, 4 * t + 2 * g + d + 2)
                            act.activation(th[:, g, d, :], ps[:, 2 + 2 * g + d, :], ACT.Tanh, scale=0.5,
                                           bias=hbias[:, bass.ds((2 * g + d) * KD + t, 1)]).then_inc(lt_done, 1)
                    act.wait_ge(lt_done, 4 * t + 3)
                    for d in range(2):
                        act.activation(la[:, d, :], th[:, 0, d, :], ACT.Exp,
                                       scale=sp[:, 1, bass.ds(d * KD + t, 1)],
                                       bias=sp[:, 1, bass.ds(d * KD + t, 1)]).then_inc(la_done, 1)
                    for d in range(2):
                        act.activation(lw[:, d, :], th[:, 0, d, :], ACT.Tanh,
                                       scale=sp[:, 2, bass.ds(d * KD + t, 1)],
                                       bias=sp[:, 2, bass.ds(d * KD + t, 1)]).then_inc(lw_done, 1)
                    if more:
                        u(i, j + 1)
                    act.wait_ge(lw_done, 2 * t + 2)
                    act.activation(lr[:], lw[:], ACT.Sqrt, scale=0.25).then_inc(lsq_done, 1)

                u(0, 0)
                with act.Fori(0, KD // 2 - 1) as i:
                    lru(i, 0, True)
                    lru(i, 1, True)
                lru(KD // 2 - 1, 0, True)
                lru(KD // 2 - 1, 1, False)

            def odd(n0):
                for m in range(2, 6):
                    split(KD, Slot(n0, 0, 2, m))

                def front(i, b):
                    h = 2 * i + b
                    used(Slot(n0, i, 10, 5 * b))
                    act.wait_ge(a_diag_mm, h + 1)
                    act.activation(hq[:], ps[:, 0, :], ACT.Sigmoid).then_inc(a_sig, 1)
                    for d in range(2):
                        used(Slot(n0, i, 10, 5 * b + 1 + d))
                        act.activation(TA[:, d, :], ps[:, 1 + d, :], ACT.Sigmoid).then_inc(a_sig, 1)
                    used(Slot(n0, i, 10, 5 * b + 4))
                    act.wait_ge(mix_done, MIX_EVEN + h - 1)
                    act.activation(hgs[:, b % 2, :], ps[:, 4, :], ACT.Sigmoid).then_inc(a_sig, 1)
                    act.activation(hi_[:], ps[:, 3, :], ACT.Copy).then_inc(a_i, 1)

                def mix(i, b, more):
                    h = 2 * i + b

                    def ahead(k):
                        split(KD, Slot(n0, i, 10, 5 * b + 5 + k + 1))

                    act.wait_ge(a_vt_mm, h + 1)
                    act.activation(hvt[:], blocks(ps[:, 3, :]), ACT.Copy).then_inc(a_vt, 1)
                    ahead(0)
                    for l in range(LEVELS):
                        if l == 0:
                            act.wait_ge(a_kq, h + 1)
                        else:
                            act.wait_ge(a_up, LEVELS * h + l)
                        if l >= 2:
                            act.wait_ge(a_lv_mm, LEVELS * h + l - 1)
                        KQ_l = KQ[:, l % 2, :, :]
                        act.activation(halves(KQ_l, 1 << l)[0], halves(Lo[:], 1 << l)[0], ACT.Copy)
                        act.activation(halves(KQ_l, 1 << l)[1], halves(Up[:], 1 << l)[1], ACT.Copy).then_inc(a_cp, 1)
                        if l in AHEAD:
                            ahead(AHEAD.index(l) + 1)
                    if more:
                        act.preload_act_table(ACT.Sigmoid)
                    act.wait_ge(a_off_mm, h + 1)
                    act.activation(hat[:, 1, :, :], blocks(ps[:, 5, :]), ACT.Copy).then_inc(a_off, 1)
                    if more:
                        front(i, b + 1)
                    ln_and_exp()
                    act.wait_ge(a_pv, h + 2)
                    act.activation(hsq[:], ps[:, 7, :], ACT.Square).then_inc(a_sq, 1)
                    act.wait_ge(a_vin, h + 2)
                    act.activation(hrs[:], hrs[:], ACT.Ln).then_inc(a_rstd, 1)
                    act.wait_ge(a_rstd, 2 * h + 1)
                    act.activation(hrs[:], hrs[:], ACT.Exp, scale=-0.5).then_inc(a_rstd, 1)

                front(0, 0)
                with act.Fori(0, HG // 2 - 1) as i:
                    mix(i, 0, True)
                    mix(i, 1, True)
                mix(HG // 2 - 1, 0, True)
                mix(HG // 2 - 1, 1, False)
                n1 = n0 + 5 * HG

                def ret(r, more):
                    c = NH + r

                    def sl(m):
                        return Slot(n1, r, 8, m)

                    act.wait_ge(rvt_mm, HT * r + 1)
                    used(sl(4))
                    act.activation(rv[:], ps[:, 4, :], ACT.Copy).then_inc(rv_ev, 1)
                    split(KD, sl(6))
                    split(KD, sl(7))
                    act.wait_ge(rvt_mm, HT * r + 2)
                    act.activation(rvt[:, :, 0, :], blocks(ps[:, 5, :]), ACT.Copy).then_inc(rvt_ev, 1)
                    act.activation(rv[:], ps[:, 0, :], ACT.Copy).then_inc(rv_ev, 1)
                    split(KD, sl(8))
                    act.wait_ge(mix_done, MIX_EVEN + HG + r)
                    for z in range(HT):
                        used(sl(6 + z))
                        act.activation(rzs[:, z, :], ps[:, 1 + z, :], ACT.Sigmoid).then_inc(rz_ev, 1)
                    act.wait_ge(rvt_mm, HT * r + 3)
                    act.activation(rvt[:, :, 1, :], blocks(ps[:, 5, :]), ACT.Copy).then_inc(rvt_ev, 1)
                    act.wait_ge(pv_mm, c + 1)
                    act.activation(rhv[:], ps[:, 3:5, :], ACT.Copy).then_inc(hv_done, 1)
                    if more:
                        split(KD, sl(9))
                    head_square(c, rhv, rq[:])
                    if more:
                        split(KD, sl(10))
                    head_rstd(c, rrec[:])
                    if more:
                        split(KD, sl(11))
                        split(KD, sl(12))
                        split(KD, sl(13))

                with act.Fori(0, NH - 1) as r:
                    ret(r, True)
                ret(NH - 1, False)

            act.sem_inc(hi_done, 2)
            for s in (lu_ev, gelu_done, lt_done, a_off, rvt_ev):
                act.sem_inc(s, 1)
            split(KD, Slot(0, 0, 2, 0))
            act.wait_ge(x_in, 16)
            for k in range(KD):
                act.activation(xh[:, k, :], x[:, k, :], ACT.Copy).then_inc(xh_done, 1)
            split(KD, Slot(0, 0, 2, 1))
            act.wait_ge(const_in, 16 * 7)
            lam = vc("lam", 0, 2 * KD)
            act.activation(sp[:, 1, :], lam, ACT.Abs).then_inc(prep_a, 1)
            act.wait_ge(prep_a, 1)
            act.activation(sp[:, 1, :], sp[:, 1, :], ACT.Exp, scale=-1.0).then_inc(prep_a, 1)
            act.wait_ge(prep_a, 2)
            act.activation(sp[:, 1, :], sp[:, 1, :], ACT.Ln, bias=1.0).then_inc(prep_a, 1)
            act.wait_ge(prep_d, 1)
            act.activation(lb[:, 0:2, :], lb[:, 0:2, :], ACT.Exp).then_inc(prep_a, 1)
            for st, (kind, n0, fi) in enumerate(stages):
                more = st < len(stages) - 1
                if kind == "ffn":
                    ffn(fi, n0, more)
                elif kind == "even":
                    even(n0)
                    out_splits(n0 + EV_SLOTS, KD, more)
                else:
                    odd(n0)
                    out_splits(n0 + OD_SLOTS, KD, more)
                layer_norm(st)

        @block.vector
        def _(dve):
            steps = [0]

            def step(ins, n=None):
                steps[0] += 1
                ins.then_inc(step_done, 1)
                dve.wait_ge(step_done, steps[0] + loop[0])

            loop = [0]

            class passes:

                def __init__(self, var, n, per):
                    self.var, self.n, self.per = var, n, per

                def __enter__(self):
                    loop[0], self.at = self.per * self.var, steps[0]

                def __exit__(self, *_):
                    assert steps[0] - self.at == self.per, (steps[0] - self.at, self.per)
                    steps[0] += self.per * (self.n - 1)
                    loop[0] = 0

            def ffn(fi, n0):
                n_ = FT // 2
                with dve.Fori(0, n_) as i, passes(i, n_, 2):
                    for b in range(2):
                        j = 2 * i + b
                        dve.wait_ge(silu_done, FT * fi + j + 1)
                        dve.wait_ge(w_used, Slot(n0, i, 4, 2 * b + 1).n + 3)
                        dve.scalar_tensor_tensor(hf[:, b, :], sg[:, b, :], 0.5, ps[:, 2 * b + 1, :], ALU.mult,
                                                 ALU.mult).then_inc(glu_done, 1)
                        dve.wait_ge(glu_done, FT * fi + j + 3)
                        hh_j = hh[:, bass.ds(j, 1), :].rearrange("p a t -> p (a t)")
                        step(dve.tensor_copy(hh_j, hf[:, b, :]))
                        dve.tensor_tensor(hl[:, bass.ds(j, 1), :].rearrange("p a t -> p (a t)"), hf[:, b, :],
                                          hh_j.bitcast(F32), ALU.subtract).then_inc(h_done, 1)

            def residual(ln, n0):
                S, Q, sq = (lt[:, k, :] for k in range(3))
                c = ps[:, 6, :]
                for k in range(2):
                    dve.wait_ge(w_used, Slot(n0, 0, 4, 2 * k + 1).n + 3)
                    dve.scalar_tensor_tensor(x[:, k, :], x[:, k, :], ALPHA, ps[:, 4 + k, :], ALU.mult,
                                             ALU.add).then_inc(y_done, 1)
                dve.wait_ge(mean_mm, 2 * ln + 1)
                dve.tensor_tensor(x[:, 0, :], x[:, 0, :], c, ALU.subtract)
                step(dve.tensor_tensor(x[:, 1, :], x[:, 1, :], c, ALU.subtract))
                dve.tensor_tensor(S, x[:, 0, :], x[:, 1, :], ALU.add).then_inc(sum_done, 1)
                dve.tensor_tensor(sq, x[:, 0, :], x[:, 0, :], ALU.mult)
                step(dve.tensor_tensor(Q, x[:, 1, :], x[:, 1, :], ALU.mult))
                dve.tensor_tensor(Q, Q, sq, ALU.add).then_inc(sq_done, 1)
                n_ = KD // 2 - 1
                with dve.Fori(0, n_) as i, passes(i, n_, 4):
                    for b in range(2):
                        k = 2 * i + b + 2
                        x_k = x[:, bass.ds(k, 1), :].rearrange("p a t -> p (a t)")
                        step(dve.scalar_tensor_tensor(x_k, x_k, ALPHA, c, ALU.mult, ALU.subtract))
                        dve.wait_ge(w_used, Slot(n0, i, 4, 2 * b + 5).n + 3)
                        dve.tensor_tensor(x_k, x_k, ps[:, 4 + b, :], ALU.add).then_inc(y_done, 1)
                        dve.wait_ge(y_done, KD * ln + k + 3)
                        dve.wait_ge(sum_done, (KD - 1) * ln + k - 1)
                        dve.tensor_tensor(S, S, x_k, ALU.add).then_inc(sum_done, 1)
                        dve.wait_ge(sq_done, (KD - 1) * ln + k - 1)
                        step(dve.tensor_tensor(sq, x_k, x_k, ALU.mult))
                        dve.tensor_tensor(Q, Q, sq, ALU.add).then_inc(sq_done, 1)

            def layer_norm(ln):
                def sub(k):
                    return dve.tensor_tensor(x[:, k, :], x[:, k, :], lt[:, 0, :], ALU.subtract)

                dve.wait_ge(m_done, ln + 1)
                sub(0)
                dve.wait_ge(msq_done, ln + 1)
                dve.wait_ge(var_mm, ln + 1)
                dve.scalar_tensor_tensor(lt[:, 3, :], ps[:, 7, :], EPS, lt[:, 2, :], ALU.add,
                                         ALU.subtract).then_inc(var_in, 1)
                sub(1)
                step(sub(2))
                dve.wait_ge(rstd_done, 2 * ln + 2)
                for k in range(KD):
                    if 3 <= k < KD - POOL_SUBS:
                        step(sub(k))
                    if k >= KD - POOL_SUBS:
                        dve.wait_ge(sub_done, POOL_SUBS * ln + k - (KD - POOL_SUBS) + 1)
                    dve.tensor_tensor(x[:, k, :], x[:, k, :], lt[:, 3, :], ALU.mult).then_inc(scaled, 1)
                    if k not in BY_ACT:
                        dve.wait_ge(scaled, KD * ln + k + 1)
                        dve.tensor_scalar(x[:, k, :], x[:, k, :], vc("ln_g", ln * KD + k), vc("ln_b", ln * KD + k),
                                          ALU.mult, ALU.add).then_inc(x_dve, 1)
                    if k - 2 in LOW_DVE and ln < len(stages) - 1:
                        low_of_x(ln + 1, k - 2)
                if ln < len(stages) - 1:
                    for k in range(KD - 2, KD):
                        if k in LOW_DVE:
                            low_of_x(ln + 1, k)
                dve.wait_ge(scaled, KD * (ln + 1))

            def low_of_x(n, k):
                dve.wait_ge(xh_done, KD * n + k + 1)
                dve.tensor_tensor(xl[:, k, :], x[:, k, :], xh[:, k, :].bitcast(F32), ALU.subtract).then_inc(xl_dve, 1)

            def head_cen(c, bank, v):
                dve.wait_ge(hmean_mm, c + 1)
                dve.tensor_tensor(v[:], v[:], ps[:, bank, None, :].to_broadcast([P, HT, T]),
                                  ALU.subtract).then_inc(hcen_done, 1)

            def head_norm(c, bank, v, r, g, tile, z_, yh, yl):
                dve.wait_ge(hvar_mm, c + 1)
                dve.tensor_scalar(r, ps[:, bank, :], EPS, None, ALU.add).then_inc(hvar_in, 1)
                dve.wait_ge(hrstd_done, 2 * c + 2)
                step(dve.tensor_tensor(v[:], v[:], r[:, None, :].to_broadcast([P, HT, T]), ALU.mult))
                for z in range(HT):
                    ins = dve.scalar_tensor_tensor(v[:, z, :], v[:, z, :], vc(g, tile + z), z_[:, z, :], ALU.mult,
                                                   ALU.mult)
                step(ins)
                y_h = yh[:, bass.ds(tile, HT), :]
                step(dve.tensor_copy(y_h, v[:]))
                dve.tensor_tensor(yl[:, bass.ds(tile, HT), :], v[:], y_h.bitcast(F32),
                                  ALU.subtract).then_inc(mix_done, 1)

            def conv(src, dst, w, b, t):
                for j in range(4):
                    wj = vc(w, KD * j + t)
                    if j:
                        ins = dve.scalar_tensor_tensor(dst[:], src[:, :, j:j + L], wj, dst[:], ALU.mult, ALU.add)
                    elif b:
                        ins = dve.tensor_scalar(dst[:], src[:, :, 0:L], wj, vc(b, t), ALU.mult, ALU.add)
                    else:
                        ins = dve.tensor_scalar(dst[:], src[:, :, 0:L], wj, None, ALU.mult)
                    if j < 3:
                        step(ins)
                return ins

            def even(n0):
                dve.memset(um[:], 0.0).then_inc(um_zero, 1)
                for t in range(KD):
                    if t >= 1:
                        dve.wait_ge(v_mm, t)
                    for j in range(3):
                        ins = dve.tensor_tensor(bd[:, j, :].rearrange("p (b d) -> p b d", d=4),
                                                w4[:, j, t, None, :].to_broadcast([P, 32, 4]),
                                                cn("bd")[:, :, None].to_broadcast([P, 32, 4]), ALU.mult)
                    ins.then_inc(bd_done, 1)
                    dve.wait_ge(u_ev, t + 1)
                    if t >= 1:
                        dve.wait_ge(c_done, t)
                    conv(um[:, t % 2], cv, "ml_cw", None, t).then_inc(c_lin, 1)
                dve.wait_ge(rows_a, 7)
                dve.memset(one[:], 1.0)
                step(dve.scalar_tensor_tensor(gf[:], gf[:], 0.0, g2[:], ALU.min, ALU.subtract))

                def scan(dst, d0, d1, op0, op1):
                    for q in range(SEQS):
                        for d in range(2):
                            def way(t_):
                                return t_ if d == 0 else t_[:, ::-1]
                            c = slice(q * L, (q + 1) * L)
                            ins = dve.tensor_tensor_scan(way(dst[:, d, c]), way(d0(d, c)), way(d1(d, c)), 0.0, op0, op1)
                    return ins

                step(scan(g2, lambda d, c: one[:], lambda d, c: gf[:, d, c], ALU.mult, ALU.add))
                dve.tensor_tensor(gi[:], gi[:], g2[:], ALU.subtract).then_inc(g_done, 1)
                dve.wait_ge(g_done, 1)
                step(scan(g1, lambda d, c: gi[:, d, c], lambda d, c: gi[:, d, c], ALU.max, ALU.max))
                step(dve.tensor_scalar(negM[:], g1[:], -1.0, None, ALU.mult))
                step(dve.tensor_tensor(g1[:], negM[:], g2[:], ALU.subtract))
                dve.tensor_scalar(g1[:], g1[:], 88.0, None, ALU.min).then_inc(marg_done, 1)
                dve.wait_ge(gT_ev, 1)
                for h in range(NH):
                    for d, E in enumerate((Ef, Eb)):
                        dve.wait_ge(mb_mm, 2 * h + d + 1)
                        for q in range(SEQS):
                            own_, other = (0, 1) if d == 0 else (1, 0)
                            full, part = gT[:, d, q * SB + own_, h:h + 1], gT[:, d, q * SB + other, h:h + 1]
                            dve.scalar_tensor_tensor(E[:, q, 0:L], ps[:, 2 + d, q * L:(q + 1) * L], full,
                                                     tri[:, d * L:(d + 1) * L], ALU.add, ALU.min)
                            o = q * L + (P if d == 0 else 0)
                            m = 0 if d == 0 else L + P
                            ins = dve.scalar_tensor_tensor(E[:, q, L:L + P], ps[:, 2 + d, o:o + P], part,
                                                           tri[:, m:m + P], ALU.add, ALU.min)
                        ins.then_inc(t_done, 1)
                    dve.wait_ge(qk_mm, h + 1)
                    for d, E in enumerate((Ef, Eb)):
                        dve.wait_ge(e_done, 2 * h + d + 1)
                        o1, o2 = (0, L + P) if d == 0 else (L, 0)
                        dve.tensor_tensor(E[:, :, 0:L], E[:, :, 0:L], ps[:, 6:8, o1:o1 + L], ALU.mult)
                        dve.tensor_tensor(E[:, :, L:L + P], E[:, :, L:L + P], ps[:, 6:8, o2:o2 + P],
                                          ALU.mult).then_inc(s_done, 1)
                    if h >= 1:
                        head_cen(h - 1, 5, hv)
                    for d, E in enumerate((Ef, Eb)):
                        dve.wait_ge(abs_done, 2 * h + d + 1)
                        dve.tensor_tensor(rec[:, d, :], rec[:, d, :], dab[:], ALU.max).then_inc(dmax_done, 1)
                        dve.wait_ge(dmax_done, 2 * h + d + 1)
                        step(dve.reciprocal(rec[:, d, :], rec[:, d, :]))
                        r = seqs(rec[:, d, :])
                        if d == 0:
                            dve.tensor_tensor(att[:, :, 0, :], E[:, :, 0:L], r, ALU.mult)
                            step(dve.tensor_tensor(att[:, :, 1, P:L], E[:, :, L:L + P], r[:, :, P:L], ALU.mult))
                        else:
                            dve.tensor_tensor(att[:, :, 1, 0:P], E[:, :, 0:P], r[:, :, 0:P], ALU.mult)
                            dve.tensor_tensor(E[:, :, P:L], E[:, :, P:L], r[:, :, P:L], ALU.mult)
                            step(dve.tensor_tensor(E[:, :, L:L + P], E[:, :, L:L + P], r[:, :, 0:P], ALU.mult))
                            dve.tensor_tensor(att[:, :, 1, P:L], att[:, :, 1, P:L], E[:, :, P:L], ALU.add)
                            dve.tensor_tensor(att[:, :, 0, 0:P], att[:, :, 0, 0:P], E[:, :, L:L + P],
                                              ALU.add).then_inc(att_done, 1)
                    if h >= 1:
                        head_norm(h - 1, 5, hv, rs[:], "ml_g", HT * (h - 1), zs, yhA, ylA)
                head_cen(NH - 1, 5, hv)
                head_norm(NH - 1, 5, hv, rs[:], "ml_g", HT * (NH - 1), zs, yhA, ylA)

                dve.memset(lbd[:], 0.0)
                dve.memset(lum[:], 0.0).then_inc(lzero, 1)
                def taps(t):
                    dve.wait_ge(lu_ev, t + 2)
                    dve.wait_ge(lg_mm, 4 * t + 1)
                    conv(lum, lx, "lru_cw", "lru_cb", t).then_inc(lx_done, 1)

                def scans(t):
                    dve.wait_ge(lsq_done, t + 1)
                    step(dve.scalar_tensor_tensor(lq[:], la[:], 1.0, lr[:], ALU.add, ALU.mult))
                    step(dve.tensor_tensor(lq[:], lq[:], lix[:], ALU.mult))
                    for q in range(SEQS):
                        c = slice(q * L, (q + 1) * L)
                        dve.tensor_tensor_scan(lw[:, 0, c], la[:, 0, c], lq[:, 0, c], 0.0, ALU.mult, ALU.add)
                        ins = dve.tensor_tensor_scan(lw[:, 1, c][:, ::-1], la[:, 1, c][:, ::-1],
                                                     lq[:, 1, c][:, ::-1], 0.0, ALU.mult, ALU.add)
                    step(ins)
                    step(dve.tensor_tensor(lw[:, 0, :], lw[:, 0, :], lw[:, 1, :], ALU.add))
                    step(dve.tensor_tensor(lw[:, 0, :], lw[:, 0, :], lgl[:], ALU.mult))
                    y_h = yhB[:, bass.ds(t, 1), :].rearrange("p a t -> p (a t)")
                    step(dve.tensor_copy(y_h, lw[:, 0, :]))
                    dve.tensor_tensor(ylB[:, bass.ds(t, 1), :].rearrange("p a t -> p (a t)"), lw[:, 0, :],
                                      y_h.bitcast(F32), ALU.subtract).then_inc(mix_done, 1)

                def gated(t):
                    dve.wait_ge(lt_done, 4 * t + 5)
                    x_ = lx[:].rearrange("p s t -> p (s t)")[:, None, :].to_broadcast([P, 2, T])
                    dve.scalar_tensor_tensor(lix[:], th[:, 1, :, :], 1.0, x_, ALU.add, ALU.mult).then_inc(lix_done, 1)
                    dve.wait_ge(lix_done, t + 2)

                taps(0)
                with dve.Fori(0, KD - 1) as t, passes(t, KD - 1, 9):
                    gated(t)
                    taps(t + 1)
                    scans(t)
                gated(KD - 1)
                scans(KD - 1)

            def odd(n0):
                def front(h, par):
                    dve.wait_ge(a_sig, 4 * h + 1)
                    dve.tensor_tensor(hq[:], hq[:], ps[:, 0, :], ALU.mult).then_inc(a_q, 1)
                    dve.wait_ge(a_sig, 4 * h + 3)
                    dve.wait_ge(a_off, h + 1)
                    step(dve.tensor_scalar(TA[:, 0:2, :], TA[:, 0:2, :], lb[:, 1, bass.ds(h, 1)],
                                           lb[:, 0, bass.ds(h, 1)], ALU.mult, ALU.add))
                    dve.tensor_copy(TA[:, 2, :], TA[:, 0, :])
                    dve.tensor_scalar(Lo[:, 0, :], TA[:, 0, :], -1.0, 1.0, ALU.mult, ALU.add)
                    dve.tensor_scalar(Up[:, 0, :], TA[:, 1, :], -1.0, 1.0, ALU.mult, ALU.add)
                    dve.wait_ge(a_q, h + 1)
                    dve.tensor_tensor(Lo[:, 1, :], hq[:], TA[:, 1, :], ALU.mult)
                    step(dve.tensor_tensor(Up[:, 1, :], hq[:], TA[:, 0, :], ALU.mult))
                    dve.tensor_tensor(ks[:], Lo[:, 0, :], Up[:, 0, :], ALU.add).then_inc(a_kq, 1)
                    dve.wait_ge(a_sig, 4 * h + 4)
                    dve.tensor_tensor(hgs[:, par, :], hgs[:, par, :], ps[:, 4, :], ALU.mult).then_inc(a_g, 1)

                def mix(i, b, more):
                    h = 2 * i + b
                    dve.wait_ge(a_diag_mm, h + 2)
                    dve.wait_ge(a_pv, h + 1)
                    dve.tensor_tensor(hat[:, 0, :, :], blocks(ps[:, 5, :]), ident[:, None, :].to_broadcast([P, NB, P]),
                                      ALU.mult).then_inc(a_diag, 1)
                    dve.wait_ge(a_diag, h + 1)

                    def pred(l):
                        dve.copy_predicated(hat[:, 0, :, :], pmask[:, l, None, :].to_broadcast([P, NB, P]),
                                            blocks(ps[:, 6 - l % 2, :])).then_inc(a_pred, 1)
                        dve.wait_ge(a_pred, LEVELS * h + l + 1)

                    for l in range(LEVELS):
                        B, cur, nxt_ = 1 << l, (TA, TB)[l % 2], (TB, TA)[l % 2]
                        n = T // B
                        dve.wait_ge(a_cp, LEVELS * h + l + 1)
                        pairs = cur[:, :, 0:n].rearrange("p r (n two) -> p r n two", two=2)
                        low, high = pairs[:, :, :, 0], pairs[:, :, :, 1]
                        lo_, up_ = halves(Lo[:], B)[0], halves(Up[:], B)[1]
                        dve.tensor_tensor(lo_, lo_, spread(high[:, 0:2, :], B), ALU.mult)
                        if l == LEVELS - 1:
                            dve.wait_ge(a_lv_mm, LEVELS * h + l)
                        dve.tensor_tensor(up_, up_, spread(low[:, 1:3, :], B), ALU.mult).then_inc(a_up, 1)
                        if l < LEVELS - 1:
                            if l >= 1:
                                dve.wait_ge(a_lv_mm, LEVELS * h + l)
                            ins = dve.tensor_tensor(nxt_[:, :, 0:n // 2], low, high, ALU.mult)
                            if l == 0:
                                step(ins)
                        if l >= 1:
                            pred(l - 1)
                    dve.wait_ge(a_lv_mm, LEVELS * h + LEVELS)
                    dve.memset(lb[:, 2, 0:1], 0.0)
                    pred(LEVELS - 1)
                    if more:
                        front(h + 1, 1 - b)
                    dve.wait_ge(a_var, h + 1)
                    dve.tensor_scalar(hrs[:], ps[:, 6, :], EPS, None, ALU.add).then_inc(a_vin, 1)
                    dve.wait_ge(a_rstd, 2 * h + 2)
                    step(dve.scalar_tensor_tensor(ho[:], ps[:, 7, :], vc("hg_g", h), hrs[:], ALU.mult, ALU.mult))
                    step(dve.tensor_tensor(ho[:], ho[:], hgs[:, b, :], ALU.mult))
                    y_h = yhA[:, bass.ds(h, 1), :].rearrange("p a t -> p (a t)")
                    step(dve.tensor_copy(y_h, ho[:]))
                    dve.tensor_tensor(ylA[:, bass.ds(h, 1), :].rearrange("p a t -> p (a t)"), ho[:],
                                      y_h.bitcast(F32), ALU.subtract).then_inc(mix_done, 1)

                n_ = HG // 2 - 1
                front(0, 0)
                with dve.Fori(0, n_) as i, passes(i, n_, 12):
                    mix(i, 0, True)
                    mix(i, 1, True)
                mix(n_, 0, True)
                mix(n_, 1, False)
                n1 = n0 + 5 * HG

                def rope(r, bank, dst, done, m):
                    dve.wait_ge(w_used, m.n + 3)
                    t1, t2 = seqs(ps[:, bank, :]), seqs(ps[:, bank + 1, :])
                    co, si = (v[:, None, :].to_broadcast([P, SEQS, L]) for v in (cos, sin))
                    for k, (t_, v) in enumerate(((t1, co), (t2, si), (t1, si), (t2, co))):
                        ins = dve.tensor_tensor(seqs(rt[:, k, :]), t_, v, ALU.mult)
                    step(ins)
                    dve.tensor_tensor(dst[:, 0, :], rt[:, 0, :], rt[:, 1, :], ALU.subtract)
                    dve.tensor_tensor(dst[:, 1, :], rt[:, 2, :], rt[:, 3, :], ALU.add).then_inc(done, 1)
                    dve.wait_ge(done, r + 1)

                dve.wait_ge(odd_in, 16)

                def ret(r):
                    c = NH + r
                    dve.wait_ge(hvar_mm, c)
                    rope(r, 0, rq, r_q, Slot(n1, r, 8, 1))
                    rope(r, 2, rk, r_k, Slot(n1, r, 8, 3))
                    dve.wait_ge(rqk_mm, r + 1)
                    dve.wait_ge(pv_mm, c)
                    for st in range(SB):
                        decay = odc[:, bass.ds(2 * L + 3 * P * r + P * (1 - st), L)]
                        ins = dve.tensor_tensor(ratt[:, :, st, :], ps[:, 6:8, st * L:(st + 1) * L],
                                                decay[:, None, :].to_broadcast([P, SEQS, L]), ALU.mult)
                    ins.then_inc(ratt_done, 1)
                    for z in range(HT):
                        dve.wait_ge(rz_ev, HT * r + z + 1)
                        dve.tensor_tensor(rzs[:, z, :], rzs[:, z, :], ps[:, 1 + z, :], ALU.mult).then_inc(rz_done, 1)
                    head_cen(c, 6, rhv)
                    head_norm(c, 7, rhv, rrec[:], "ret_g", HT * r, rzs, yhB, ylB)

                with dve.Fori(0, NH) as r, passes(r, NH, 5):
                    ret(r)

            dve.sem_inc(glu_done, 2)
            dve.sem_inc(a_vin, 1)
            dve.sem_inc(lix_done, 1)
            dve.wait_ge(x_in, 16)
            for k in LOW_DVE:
                low_of_x(0, k)
            dve.sem_inc(y_done, 2)
            dve.wait_ge(const_in, 16 * 7)
            l0, l1 = vc("lb", 0, KD), vc("lb", KD, KD)
            step(dve.tensor_tensor(lb[:, 2, :], l0, l1, ALU.max))
            dve.tensor_copy(pmask[:], mask_f[:])
            dve.tensor_tensor(lb[:, 0, :], l0, lb[:, 2, :], ALU.subtract)
            dve.tensor_tensor(lb[:, 1, :], l1, lb[:, 2, :], ALU.subtract).then_inc(prep_d, 1)
            dve.tensor_scalar(hbias[:], vec[:, bass.ds(VEC["b_a"][0], 4 * KD)], 0.5, None, ALU.mult)
            dve.wait_ge(prep_a, 3)
            step(dve.tensor_scalar(sp[:, 2, :], vc("lam", 0, 2 * KD), -1.0, 0.0, ALU.mult, ALU.max))
            step(dve.tensor_tensor(sp[:, 0, :], sp[:, 2, :], sp[:, 1, :], ALU.add))
            dve.tensor_scalar(sp[:, 1, :], sp[:, 0, :], -4.0, None, ALU.mult)
            dve.tensor_scalar(sp[:, 2, :], sp[:, 0, :], 2.0, None, ALU.mult)
            dve.wait_ge(prep_a, 4)
            step(dve.tensor_tensor(lb[:, 2, :], lb[:, 0, :], lb[:, 1, :], ALU.add))
            step(dve.reciprocal(lb[:, 2, :], lb[:, 2, :]))
            step(dve.tensor_tensor(lb[:, 0, :], lb[:, 1, :], lb[:, 2, :], ALU.mult))
            step(dve.tensor_scalar(lb[:, 1, :], lb[:, 0, :], -1.0, 1.0, ALU.mult, ALU.add))
            for st, (kind, n0, fi) in enumerate(stages):
                if kind == "ffn":
                    ffn(fi, n0)
                elif kind == "even":
                    even(n0)
                else:
                    odd(n0)
                residual(st, n0 + own[kind])
                layer_norm(st)


def _host_constants():
    s, t = np.arange(P)[:, None], np.arange(P)[None, :]
    con = np.zeros((P, NC), np.float32)

    def put(name, v):
        o, n = CON[name]
        con[:, o:o + n] = v

    put("ident", s == t)
    put("mean_d", 1.0 / D)
    put("mean_256", 1.0 / (HT * P))
    put("mean_128", 1.0 / P)
    put("ones", 1.0)
    tri = np.zeros((P, 2 * L), np.float32)
    tri[:, 0:P][s > t] = -1e30
    tri[:, L + P:][s < t] = -1e30
    put("tri", tri)
    put("bd", np.arange(P)[:, None] // 4 == np.arange(32)[None, :])
    pmask = np.zeros((P, LEVELS, P), np.float32)
    for l in range(LEVELS):
        pmask[:, l, :] = (s >> (l + 1) == t >> (l + 1)) & (s >> l != t >> l)
    sel = np.zeros((NH, NH, P), np.float32)
    for h in range(NH):
        sel[h, h, :] = 1.0
    half = HT * P // 2
    ang = np.arange(L, dtype=np.float64)[None, :] * 10000.0 ** (-np.arange(half, dtype=np.float64)[:, None] / half)
    lg = np.log(1.0 - 2.0 ** (-5.0 - np.arange(NH, dtype=np.float64)))
    decay = np.zeros((NH, P, 3 * P))
    for h in range(NH):
        def both(diff):
            fwd = np.where(diff >= 0, np.exp(np.minimum(diff * lg[h], 0.0)), 0.0)
            bwd = np.where(diff <= 0, np.exp(np.minimum(-diff * lg[NH - 1 - h], 0.0)), 0.0)
            return (fwd + bwd) / np.sqrt(HT * P)
        decay[h] = np.concatenate([both((t - s) * 1.0 - P), both((t - s) * 1.0), both((t - s) * 1.0 + P)], 1)
    odc = np.concatenate([np.cos(ang), np.sin(ang), decay.transpose(1, 0, 2).reshape(P, -1)], 1).astype(np.float32)
    return con, pmask, sel, odc


def _layout(v):
    def cols(w):
        return np.asarray(w).reshape(-1, P).T

    def slots(w, kh, tiles):
        k, m = w.shape
        w = w.reshape(kh, k // P // kh, P, m // P, P).transpose(3, 0, 2, 1, 4)[tiles]
        return w.reshape(len(tiles) * kh, P, -1)

    v = {k: np.asarray(w) for k, w in v.items()}
    x_in = np.concatenate([v["x_prompt"][0], v["x_sample"][0]], 0).T.reshape(KD, P, T)
    ffn = [(v["ffn_a_w_in"][0], v["ffn_a_w_out"][0]), (v["ffn_b_w_in"][0], v["ffn_b_w_out"][0]),
           (v["ffn_a_w_in"][1], v["ffn_a_w_out"][1]), (v["ffn_b_w_in"][1], v["ffn_b_w_out"][1])]
    pairs = [t for j in range(FT) for t in (j, FT + j)]
    ev = list(range(2 * KD)) + [t for j in range(KD) for t in (2 * KD + j, 3 * KD + j)]
    od = [t for h in range(HG) for t in (h, KD + h, 2 * KD + h, 3 * KD + h, 4 * KD + h)]
    od += [(5 + part) * KD + HT * r + z for r in range(NH) for part in range(4) for z in range(HT)]
    every = list(range(KD))
    con, pmask, sel, odc = _host_constants()
    vec = np.concatenate([cols(v[n]) for n in (
        "ln_g", "ln_b", "ml_conv_w", "ml_conv_b", "ml_norm_g", "lru_conv_w", "lru_conv_b", "lru_b_a", "lru_b_x",
        "lru_lambda", "hg_lb_logits", "hg_norm_g", "ret_norm_g")], 1)
    w4 = np.stack([v[n].reshape(KD, P, 4) for n in ("ml_wq", "ml_wk", "ml_wv")]).transpose(2, 0, 1, 3)
    wg = np.stack([v["ml_w_ig"][0, 0], v["ml_w_fg"][0, 0], v["ml_w_ig"][0, 1], v["ml_w_fg"][0, 1]], 1)
    gb = np.stack([v["ml_b_ig"][0, 0], v["ml_b_fg"][0, 0], v["ml_b_ig"][0, 1], v["ml_b_fg"][0, 1]], 1)
    lru = np.stack([v["lru_w_a"][0, 0], v["lru_w_a"][0, 1], v["lru_w_x"][0, 0], v["lru_w_x"][0, 1]], 2)
    out = {
        "x_in": x_in, "con": con, "vec": vec, "pmask": pmask, "sel": sel, "odc": odc, "w4": w4,
        "wg": wg.reshape(3 * KD, P, 4, NH).transpose(1, 0, 2, 3), "gb": gb, "w_lru": lru,
        "w_in": np.concatenate([slots(w, 1, pairs) for w, _ in ffn]),
        "w_out": np.concatenate([slots(w, 2, every) for _, w in ffn]),
        "w_ev": slots(v["ev_w_in"][0], 1, ev), "w_evo": slots(v["ev_w_out"][0], 2, every),
        "w_od": slots(v["od_w_in"][0], 1, od), "w_odo": slots(v["od_w_out"][0], 2, every),
    }
    return {k: np.ascontiguousarray(w) for k, w in out.items()}


def kernel(**inputs):
    import concourse.bacc as bacc
    from concourse.bass_utils import run_bass_kernel_spmd

    arrays = _layout(inputs)
    nc = bacc.Bacc("TRN2", target_bir_lowering=False, num_devices=1)
    aps = {k: nc.dram_tensor(k, w.shape, mybir.dt.from_np(w.dtype), kind="ExternalInput").ap()
           for k, w in arrays.items()}
    aps["out"] = nc.dram_tensor("out", (KD, P, T), F32, kind="ExternalOutput").ap()
    build(nc, aps)
    r = run_bass_kernel_spmd(nc, [arrays], core_ids=[0])
    y = r.results[0]["out"].reshape(D, SEQS, L).transpose(1, 2, 0)
    return np.ascontiguousarray(y[0:1]), np.ascontiguousarray(y[1:2])
```
